# Optimizing a Trainium2 kernel written in Bass

```python
import jax, jax.numpy as jnp
from jax import lax
import numpy as np

D_MODEL = 1024
BATCH = 1
SEQ = 512
DEPTH = 2

N_MIXERS = 3
PL_DIM = 256
EPS = 1e-6
BLOCK = 128

SB_HEADS = 16
SB_HEAD_DIM = D_MODEL // SB_HEADS
RET_HEADS = 4
RET_QK_DIM = D_MODEL // RET_HEADS
RET_V_DIM = 2 * D_MODEL // RET_HEADS
ROPE_BASE = 10000.0
SGU_WIDTH = 2 * D_MODEL
SGU_GROUPS = 8
SGU_GROUP_DIM = SGU_WIDTH // SGU_GROUPS
FFN_DIM = 2816
CONV_WIDTH = 3

N_SB = len(range(0, DEPTH, N_MIXERS))
N_RET = len(range(1, DEPTH, N_MIXERS))
N_SGU = len(range(2, DEPTH, N_MIXERS))

kernel_name = "hybrid_stickbreak_retention_sgu_trunk"

def rmsnorm(x, g):
    xf = x.astype(jnp.float32)
    y = xf * lax.rsqrt(jnp.mean(xf * xf, axis=-1, keepdims=True) + EPS)
    return (y * g.astype(jnp.float32)).astype(x.dtype)

def stick_breaking_attention(h, w_in, w_out):
    b, s, _ = h.shape
    qkv = h @ w_in
    q, k, v = jnp.split(qkv, 3, axis=-1)
    to_heads = lambda a: a.reshape(b, s, SB_HEADS, SB_HEAD_DIM).transpose(0, 2, 1, 3)
    q, k, v = to_heads(q), to_heads(k), to_heads(v)
    scale = SB_HEAD_DIM ** -0.5
    outs = []
    for blk in range(s // BLOCK):
        t0 = blk * BLOCK
        end = t0 + BLOCK
        qb = q[:, :, t0:end]
        kb = k[:, :, :end]
        vb = v[:, :, :end]
        z = jnp.einsum("bhtd,bhsd->bhts", qb, kb).astype(jnp.float32) * scale
        t_idx = t0 + jnp.arange(BLOCK)[:, None]
        s_idx = jnp.arange(end)[None, :]
        mask = s_idx < t_idx
        log_keep = jnp.where(mask, jax.nn.log_sigmoid(-z), 0.0)
        tail = lax.cumsum(log_keep, axis=3, reverse=True)
        between = jnp.concatenate([tail[..., 1:], jnp.zeros_like(tail[..., :1])], axis=-1)
        a = jnp.where(mask, jnp.exp(jax.nn.log_sigmoid(z) + between), 0.0)
        outs.append(jnp.einsum("bhts,bhsd->bhtd", a.astype(vb.dtype), vb))
    o = jnp.concatenate(outs, axis=2).transpose(0, 2, 1, 3).reshape(b, s, D_MODEL)
    return o @ w_out

def rotary(x, pos):
    half = x.shape[-1] // 2
    inv_freq = 1.0 / (ROPE_BASE ** (jnp.arange(half, dtype=jnp.float32) / half))
    ang = pos[:, None] * inv_freq[None, :]
    cos = jnp.cos(ang).astype(x.dtype)
    sin = jnp.sin(ang).astype(x.dtype)
    x1, x2 = x[..., :half], x[..., half:]
    return jnp.concatenate([x1 * cos - x2 * sin, x2 * cos + x1 * sin], axis=-1)

def retention(h, w_in, w_out):
    b, s, _ = h.shape
    nc = s // BLOCK
    proj = h @ w_in
    q = proj[..., :D_MODEL].reshape(b, s, RET_HEADS, RET_QK_DIM).transpose(0, 2, 1, 3)
    k = proj[..., D_MODEL:2 * D_MODEL].reshape(b, s, RET_HEADS, RET_QK_DIM).transpose(0, 2, 1, 3)
    v = proj[..., 2 * D_MODEL:4 * D_MODEL].reshape(b, s, RET_HEADS, RET_V_DIM).transpose(0, 2, 1, 3)
    g = proj[..., 4 * D_MODEL:]
    pos = jnp.arange(s, dtype=jnp.float32)
    q = rotary(q, pos)
    k = rotary(k, pos) * (RET_QK_DIM ** -0.5)
    q = q.reshape(b, RET_HEADS, nc, BLOCK, RET_QK_DIM)
    k = k.reshape(b, RET_HEADS, nc, BLOCK, RET_QK_DIM)
    v = v.reshape(b, RET_HEADS, nc, BLOCK, RET_V_DIM)

    log_gamma = jnp.log1p(-jnp.exp2(-5.0 - jnp.arange(RET_HEADS, dtype=jnp.float32)))
    idx = jnp.arange(BLOCK, dtype=jnp.float32)
    rel = idx[:, None] - idx[None, :]
    decay_intra = jnp.where(rel >= 0, jnp.exp(log_gamma[:, None, None] * jnp.maximum(rel, 0.0)), 0.0)
    decay_q = jnp.exp(log_gamma[:, None] * (idx + 1.0))
    decay_k = jnp.exp(log_gamma[:, None] * (BLOCK - 1.0 - idx))
    decay_chunk = jnp.exp(log_gamma * BLOCK)

    scores = jnp.einsum("bhncd,bhnmd->bhncm", q, k).astype(jnp.float32) * decay_intra[None, :, None]
    intra = jnp.einsum("bhncm,bhnme->bhnce", scores.astype(v.dtype), v)

    k_dec = k * decay_k[None, :, None, :, None].astype(k.dtype)

    def step(state, xs):
        qc, kc, vc = xs
        inter = jnp.einsum("bhcd,bhde->bhce", qc, state)
        state = state * decay_chunk[None, :, None, None] + jnp.einsum("bhcd,bhce->bhde", kc, vc).astype(jnp.float32)
        return state, inter.astype(jnp.float32)

    state0 = jnp.zeros((b, RET_HEADS, RET_QK_DIM, RET_V_DIM), jnp.float32)
    _, inter = lax.scan(step, state0, (jnp.moveaxis(q, 2, 0), jnp.moveaxis(k_dec, 2, 0), jnp.moveaxis(v, 2, 0)))
    inter = jnp.moveaxis(inter, 0, 2) * decay_q[None, :, None, :, None]
    o = intra.astype(jnp.float32) + inter

    mu = jnp.mean(o, axis=-1, keepdims=True)
    var = jnp.mean(jnp.square(o - mu), axis=-1, keepdims=True)
    o = (o - mu) * lax.rsqrt(var + EPS)
    o = o.transpose(0, 2, 3, 1, 4).reshape(b, s, RET_HEADS * RET_V_DIM)
    y = (jax.nn.silu(g.astype(jnp.float32)) * o).astype(h.dtype)
    return y @ w_out

def chunked_sgu(h, w_in, sgu_norm, w_s, b_s, w_out):
    b, s, _ = h.shape
    nc = s // BLOCK
    z = jax.nn.gelu(h @ w_in)
    u, v = jnp.split(z, 2, axis=-1)
    v = rmsnorm(v, sgu_norm).reshape(b, nc, BLOCK, SGU_GROUPS, SGU_GROUP_DIM)
    causal = jnp.tril(jnp.ones((BLOCK, BLOCK), dtype=w_s.dtype))
    w = w_s * causal[None]
    mixed = jnp.einsum("gts,bnsgc->bntgc", w, v) + b_s.T[None, None, :, :, None]
    return (u * mixed.reshape(b, s, SGU_WIDTH)) @ w_out

def conv_gated_ffn(h, w_in, conv_w, conv_b, w_out):
    s = h.shape[1]
    a = h @ w_in
    gate, up = a[..., :FFN_DIM], a[..., FFN_DIM:]
    gpad = jnp.pad(gate, ((0, 0), (CONV_WIDTH - 1, 0), (0, 0)))
    conv = conv_b + sum(gpad[:, tap:tap + s] * conv_w[tap] for tap in range(CONV_WIDTH))
    return (jax.nn.silu(conv) * up) @ w_out

def per_layer_embed(x, p_i, norm_g, w_gate, w_proj):
    gate = jax.nn.sigmoid((rmsnorm(x, norm_g) @ w_gate).astype(jnp.float32)).astype(x.dtype)
    return x + gate * (p_i @ w_proj)

def setup_inputs(seed: int = 0) -> dict:
    key = jax.random.key(seed)
    ks = iter(jax.random.split(key, 32))
    nrm = lambda shape, fan: jax.random.normal(next(ks), shape, jnp.float32) * (fan ** -0.5)
    gain = lambda shape: 1.0 + 0.02 * jax.random.normal(next(ks), shape, jnp.float32)
    return {
        "x": jax.random.normal(next(ks), (BATCH, SEQ, D_MODEL), jnp.float32),
        "p": jax.random.normal(next(ks), (DEPTH, BATCH, SEQ, PL_DIM), jnp.float32),
        "norm_mix": gain((DEPTH, D_MODEL)),
        "norm_ffn": gain((DEPTH, D_MODEL)),
        "norm_pl": gain((DEPTH, D_MODEL)),
        "norm_final": gain((D_MODEL,)),
        "sb_w_in": nrm((N_SB, D_MODEL, 3 * D_MODEL), D_MODEL),
        "sb_w_out": nrm((N_SB, D_MODEL, D_MODEL), D_MODEL),
        "ret_w_in": nrm((N_RET, D_MODEL, 6 * D_MODEL), D_MODEL),
        "ret_w_out": nrm((N_RET, 2 * D_MODEL, D_MODEL), 2 * D_MODEL),
        "sgu_w_in": nrm((N_SGU, D_MODEL, 2 * SGU_WIDTH), D_MODEL),
        "sgu_norm": gain((N_SGU, SGU_WIDTH)),
        "sgu_w_s": nrm((N_SGU, SGU_GROUPS, BLOCK, BLOCK), BLOCK),
        "sgu_b_s": gain((N_SGU, SGU_GROUPS, BLOCK)),
        "sgu_w_out": nrm((N_SGU, SGU_WIDTH, D_MODEL), SGU_WIDTH),
        "ffn_w_in": nrm((DEPTH, D_MODEL, 2 * FFN_DIM), D_MODEL),
        "ffn_conv_w": nrm((DEPTH, CONV_WIDTH, FFN_DIM), CONV_WIDTH),
        "ffn_conv_b": 0.02 * jax.random.normal(next(ks), (DEPTH, FFN_DIM), jnp.float32),
        "ffn_w_out": nrm((DEPTH, FFN_DIM, D_MODEL), FFN_DIM),
        "pl_w_gate": nrm((DEPTH, D_MODEL, D_MODEL), D_MODEL),
        "pl_w_proj": nrm((DEPTH, PL_DIM, D_MODEL), PL_DIM),
    }

def reference(x, p, norm_mix, norm_ffn, norm_pl, norm_final, sb_w_in, sb_w_out, ret_w_in, ret_w_out,
              sgu_w_in, sgu_norm, sgu_w_s, sgu_b_s, sgu_w_out, ffn_w_in, ffn_conv_w, ffn_conv_b, ffn_w_out,
              pl_w_gate, pl_w_proj):
    for i in range(DEPTH):
        kind = i % N_MIXERS
        j = i // N_MIXERS
        h = rmsnorm(x, norm_mix[i])
        if kind == 0:
            m = stick_breaking_attention(h, sb_w_in[j], sb_w_out[j])
        elif kind == 1:
            m = retention(h, ret_w_in[j], ret_w_out[j])
        else:
            m = chunked_sgu(h, sgu_w_in[j], sgu_norm[j], sgu_w_s[j], sgu_b_s[j], sgu_w_out[j])
        x = x + m
        x = x + conv_gated_ffn(rmsnorm(x, norm_ffn[i]), ffn_w_in[i], ffn_conv_w[i], ffn_conv_b[i], ffn_w_out[i])
        x = per_layer_embed(x, p[i], norm_pl[i], pl_w_gate[i], pl_w_proj[i])
    return rmsnorm(x, norm_final)


_drawn_inputs = setup_inputs


def setup_inputs(seed=0):
    import zlib

    import numpy as np

    out = dict(_drawn_inputs(seed))
    spreads = {}
    factors = {'norm_ffn': 3.237, 'norm_pl': 8.0, 'norm_final': 2.701, 'ffn_conv_b': 4.582}
    for name, (base, spread) in spreads.items():
        noise = np.random.default_rng([zlib.crc32(name.encode()), seed]).standard_normal(out[name].shape)
        drawn = base * np.exp(spread * noise) if base else spread * noise
        out[name] = __import__('jax').numpy.asarray(drawn.astype(out[name].dtype))
    for name, factor in factors.items():
        out[name] = (out[name] * factor).astype(out[name].dtype)
    return out
```

```python
from contextlib import ExitStack

import numpy as np

import concourse.bass as bass
import concourse.mybir as mybir
from concourse.alu_op_type import AluOpType as ALU

ACT = mybir.ActivationFunctionType
F32 = mybir.dt.float32
F32R = mybir.dt.float32r

P = 128
D = 1024
T = 512
KC = D // P
TB = T // P
HEADS, HD = 16, 64
PAIRS = HEADS // 2
RH, RQK, RV = 4, 256, 512
RQC, RVC = RQK // P, RV // P
FF = 2816
FC = FF // P
FH = FC // 2
PL = 256
PC = PL // P
EPS = 1e-6
MASKED = -1e30
NORMS = 7
CONV = 3
DMA_SCRATCH = 256

ATT_TILES = 3 * PAIRS
W8 = 8
HEAD_TILES = 16
FFN_IN_TILES, FFN_OUT_TILES = 2 * FC, 2 * KC
PL_TILES = KC * PC // W8 + KC
RUNS = [
    (KC + FFN_IN_TILES, W8), (FFN_OUT_TILES, FH),
    (PL_TILES + RH * HEAD_TILES + FFN_IN_TILES, W8), (FFN_OUT_TILES, FH), (PL_TILES, W8)]
ATT_RING, RING, RAW_RING = 3, 4, 2
RAW_COLS = ATT_RING * W8 * P
assert RAW_RING * FH * P <= RAW_COLS

C_COS, C_SIN, C_DECAY = 0, T, 2 * T
C_TRI = C_DECAY + RH * T
C_ONES, C_IDENT, C_MASK = C_TRI + P, C_TRI + 2 * P, C_TRI + 3 * P
C_COLS = C_MASK + P
G_GAIN, G_CONVW = 0, NORMS * KC
G_CONVB = G_CONVW + 2 * CONV * FC
G_COLS = G_CONVB + 2 * FC


def program(nc, xT, pT, w8, w11, params, consts, outT):
    ctx = ExitStack()
    with ctx:
        def sb(name, shape, dt=F32, where=ctx):
            return where.enter_context(nc.sbuf_tensor(name, [P] + shape, dt))

        def sem(name):
            return ctx.enter_context(nc.semaphore(name))

        x = sb("x", [KC, T])
        xh, xl = sb("xh", [KC, T], F32R), sb("xl", [KC, T], F32R)
        raw = sb("raw", [RAW_COLS])
        wh, wl = sb("wh", [RING, FH * P], F32R), sb("wl", [RING, FH * P], F32R)
        par = sb("par", [G_COLS])
        eps, turn, pool_turn = sb("eps", [1]), sb("turn", [1]), sb("pool_turn", [2])
        rstd, std, square = sb("rstd", [T]), sb("std", [T]), sb("square", [T])
        sumsq = sb("sumsq", [T])
        sumsq_h, sumsq_l = sb("sumsq_h", [T], F32R), sb("sumsq_l", [T], F32R)
        negtri, negones, ident_r, maskneg, ones_r = (
            sb(n, [P], F32R) for n in ("negtri", "negones", "ident_r", "maskneg", "ones_r"))
        ident = sb("ident", [P])

        with ExitStack() as ph:
            cst = sb("cst", [C_COLS - C_TRI], F32, ph)
            tmp = sb("att_tmp", [T], F32, ph)
            vf = sb("vf", [T], F32, ph)
            qh, ql, kh, kl = (sb(n, [2, T], F32R, ph) for n in ("qh", "ql", "kh", "kl"))
            vh, vl = sb("vh", [TB, P], F32R, ph), sb("vl", [TB, P], F32R, ph)
            sp = [sb(f"sp{j}", [T - j * P], F32, ph) for j in range(TB)]
            sph = [sb(f"sph{j}", [T - j * P], F32R, ph) for j in range(TB)]
            spl = [sb(f"spl{j}", [T - j * P], F32R, ph) for j in range(TB)]
            ah = [sb(f"ah{j}", [T - j * P], F32R, ph) for j in range(TB)]
            al = [sb(f"al{j}", [T - j * P], F32R, ph) for j in range(TB)]
            oh, ol = sb("oh", [PAIRS, T], F32R, ph), sb("ol", [PAIRS, T], F32R, ph)
        with ExitStack() as ph:
            gate = sb("gate", [2, T + 2], F32, ph)
            conv, up = sb("conv", [2, T], F32, ph), sb("up", [T], F32, ph)
            yf = sb("yf", [T], F32, ph)
            yh, yl = sb("yh", [FC, T], F32R, ph), sb("yl", [FC, T], F32R, ph)
        with ExitStack() as ph:
            pin = sb("pin", [PC, T], F32, ph)
            pinh, pinl = sb("pinh", [PC, T], F32R, ph), sb("pinl", [PC, T], F32R, ph)
            proj = sb("proj", [KC, T], F32, ph)
            gated = sb("gated", [2, T], F32, ph)
            outt = sb("outt", [2, T], F32, ph)
        with ExitStack() as ph:
            ang = sb("ang", [2, T], F32, ph)
            decay = sb("decay", [RH, T], F32, ph)
            cosr, sinr = sb("cosr", [T], F32, ph), sb("sinr", [T], F32, ph)
            stdT, rstdT = sb("stdT", [TB, 2], F32, ph), sb("rstdT", [TB, 2], F32, ph)
            rot = sb("rot", [4, T], F32, ph)
            rqh, rql, rkh, rkl = (sb(n, [RQC, T], F32R, ph) for n in ("rqh", "rql", "rkh", "rkl"))
            rvh, rvl = sb("rvh", [TB, RV], F32R, ph), sb("rvl", [TB, RV], F32R, ph)
            sf = sb("sf", [T], F32, ph)
            sh = [sb(f"sh{j}", [T - j * P], F32R, ph) for j in range(TB)]
            sl = [sb(f"sl{j}", [T - j * P], F32R, ph) for j in range(TB)]
            sg = sb("sg", [RVC, T], F32, ph)
            st6 = sb("st6", [TB, nc.vector.BN_STATS_DIM], F32, ph)
            st2 = sb("st2", [TB, nc.vector.BN_AGGR_DIM], F32, ph)
            gstd, grs, gnb = sb("gstd", [TB], F32, ph), sb("grs", [TB], F32, ph), sb("gnb", [TB], F32, ph)
            on = sb("on", [TB, RV], F32, ph)
            ryf = sb("ryf", [T], F32, ph)
            ryh, ryl = sb("ryh", [RVC, T], F32R, ph), sb("ryl", [RVC, T], F32R, ph)

        bank = [ctx.enter_context(nc.psum_tensor(f"bank{i}", [P, T], F32)) for i in range(8)]
        Z, O = bank[2:6], bank[6:8]
        AUX = bank[4:6]
        STAT, STAT_T = bank[4], bank[5]

        x_loaded = [sem(f"x_loaded{k}") for k in range(KC)]
        par_loaded, cst_loaded, p_loaded, tab_loaded = (
            sem(n) for n in ("par_loaded", "cst_loaded", "p_loaded", "tab_loaded"))
        w_loaded = [sem(f"w_loaded{r}") for r in range(ATT_RING)]
        w_high, w_low, w_begun = sem("w_high"), sem("w_low"), sem("w_begun")
        chunk_done, chunk_freed = sem("chunk_done"), sem("chunk_freed")
        consts_ready, eps_ready, pads_ready = sem("consts_ready"), sem("eps_ready"), sem("pads_ready")
        turn_ready = sem("turn_ready")
        x_new, x_high, x_low, x_squared, sq_added, sumsq_zero = (
            sem(n) for n in ("x_new", "x_high", "x_low", "x_squared", "sq_added", "sumsq_zero"))
        sumsq_high, sumsq_low, stat_done, std_ready, rstd_ready = (
            sem(n) for n in ("sumsq_high", "sumsq_low", "stat_done", "std_ready", "rstd_ready"))
        statT_done, stdT_ready, rstdT_ready = sem("statT_done"), sem("stdT_ready"), sem("rstdT_ready")
        qk_high, qk_low, vt_high = sem("qk_high"), sem("qk_low"), sem("vt_high")
        z_done, z_abs, z_exp, z_ln = sem("z_done"), sem("z_abs"), sem("z_exp"), sem("z_ln")
        sp_full, sp_high, sp_low = sem("sp_full"), sem("sp_high"), sem("sp_low")
        cum_done, a_full, a_high, a_low = sem("cum_done"), sem("a_full"), sem("a_high"), sem("a_low")
        o_done, o_high, o_low = sem("o_done"), sem("o_high"), sem("o_low")
        conv_step, gate_silu, y_full, y_high, y_low = (
            sem(n) for n in ("conv_step", "gate_silu", "y_full", "y_high", "y_low"))
        p_high, p_low = sem("p_high"), sem("p_low")
        gate_open, gate_times = sem("gate_open"), sem("gate_times")
        tab_scaled, rot_parts, rot_full, rot_high, rot_low = (
            sem(n) for n in ("tab_scaled", "rot_parts", "rot_full", "rot_high", "rot_low"))
        rv_high = sem("rv_high")
        aux_done, aux_freed = sem("aux_done"), sem("aux_freed")
        s_high, s_low = sem("s_high"), sem("s_low")
        g_silu = sem("g_silu")
        ro_done, ro_stat, ro_aggr, ro_std, ro_rs, ro_nb, ro_norm = (
            sem(n) for n in ("ro_done", "ro_stat", "ro_aggr", "ro_std", "ro_rs", "ro_nb", "ro_norm"))
        ry_high, ry_low = sem("ry_high"), sem("ry_low")
        out_ready, out_stored = sem("out_ready"), [sem("out_stored0"), sem("out_stored1")]

        C_ATT = 0
        C_ATTOUT = 4 * PAIRS
        C_FFN = [C_ATTOUT + KC, 0]
        C_FFNOUT = [C_FFN[0] + 2 * FC, 0]
        C_PL = [C_FFNOUT[0] + KC, 0]
        C_RET = C_PL[0] + 2 * KC
        HEAD_CHUNKS = 2 * RQC + TB + KC + RVC
        C_FFN[1] = C_RET + RH * HEAD_CHUNKS
        C_FFNOUT[1] = C_FFN[1] + 2 * FC
        C_PL[1] = C_FFNOUT[1] + KC
        N_ATTOUT = ATT_TILES
        N_FFN = [N_ATTOUT + KC, 0]
        N_FFNOUT = [N_FFN[0] + FFN_IN_TILES, 0]
        N_PL = [N_FFNOUT[0] + FFN_OUT_TILES, 0]
        N_RET = N_PL[0] + PL_TILES
        N_FFN[1] = N_RET + RH * HEAD_TILES
        N_FFNOUT[1] = N_FFN[1] + FFN_IN_TILES
        N_PL[1] = N_FFNOUT[1] + FFN_OUT_TILES

        def gain(norm, k):
            at = G_GAIN + norm * KC + k
            return par[:, at:at + 1]

        def one(t, i):
            if isinstance(i, int):
                return t[:, i, :]
            return t[:, bass.ds(i, 1), :].rearrange("p a t -> p (a t)")

        def col(t, i):
            return t[:, i:i + 1] if isinstance(i, int) else t[:, bass.ds(i, 1)]

        block = ctx.enter_context(nc.Block())

        def raw_slot(ring, r, blocks):
            wide = RAW_COLS // ring
            return raw[:, r * wide:r * wide + blocks * P]

        @block.sync
        def _(sp_eng):
            def load(n, r, ring, blocks, src):
                sp_eng.dma_start(raw_slot(ring, r, blocks), src).then_inc(w_loaded[r], 16)

            sp_eng.dma_start(par[:], params).then_inc(par_loaded, 16)
            for k in range(KC):
                sp_eng.dma_start(x[:, k, :], xT[k]).then_inc(x_loaded[k], 16)
                if k < ATT_RING:
                    load(k, k, ATT_RING, W8, w8[k])
            sp_eng.dma_start(cst[:], consts[:, C_TRI:C_COLS]).then_inc(cst_loaded, 16)
            with sp_eng.Fori(1, PAIRS) as i:
                for u in range(ATT_RING):
                    sp_eng.wait_ge(w_low, ATT_RING * i + u - ATT_RING + 1)
                    load(0, u, ATT_RING, W8, w8[bass.ds(ATT_RING * i + u, 1)].rearrange("a p n -> (a p) n"))

            at8, at11, n0 = ATT_TILES, 0, ATT_TILES
            for run, (tiles, blocks) in enumerate(RUNS):
                src, at = (w8, at8) if blocks == W8 else (w11, at11)
                if run == 0:
                    sp_eng.wait_ge(w_low, ATT_TILES)
                def group(i, k):
                    for u in range(k):
                        n = n0 + RING * i + u
                        if not (run == 0 and isinstance(i, int) and u < RAW_RING):
                            sp_eng.wait_ge(w_low, n - RAW_RING + 1)
                        t = at + RING * i + u
                        load(n, u % RAW_RING, RAW_RING, blocks,
                             src[t] if isinstance(t, int) else src[bass.ds(t, 1)].rearrange("a p n -> (a p) n"))
                group(0, RING)
                with sp_eng.Fori(1, tiles // RING) as i:
                    group(i, RING)
                if tiles % RING:
                    group(tiles // RING, tiles % RING)
                n0 += tiles
                at8, at11 = (at8 + tiles, at11) if blocks == W8 else (at8, at11 + tiles)
            for m in range(KC):
                sp_eng.wait_ge(out_ready, m + 1)
                sp_eng.dma_start(outT[m], outt[:, m % 2, :]).then_inc(out_stored[m % 2], 16)
            for s in out_stored:
                sp_eng.wait_ge(s, 16 * KC // 2)

        @block.gpsimd
        def _(pool):
            def split(n, slot, r, ring, blocks, loads):
                src = raw_slot(ring, r, blocks)
                pool.wait_ge(w_loaded[r], 16 * loads)
                nc.gpsimd.tensor_tensor(pool_turn[:, 1:2], pool_turn[:, 0:1], pool_turn[:, 0:1], ALU.add)
                high = wh[:, slot, 0:blocks * P]
                nc.gpsimd.tensor_scalar(high, src, 1.0, None, ALU.mult).then_inc(w_high, 1)
                pool.wait_ge(w_high, n + 1)
                nc.gpsimd.tensor_tensor(wl[:, slot, 0:blocks * P], src, high.bitcast(F32), ALU.subtract)\
                    .then_inc(w_low, 1)

            nc.gpsimd.memset(pool_turn[:], 0.0).then_inc(turn_ready, 1)
            pool.wait_ge(turn_ready, 1)
            for u in range(ATT_RING):
                split(u, u, u, ATT_RING, W8, 1)
            with pool.Fori(1, PAIRS) as i:
                for u in range(ATT_RING):
                    n = ATT_RING * i + u
                    pool.wait_ge(w_begun, n - ATT_RING + 2)
                    split(n, u, u, ATT_RING, W8, i + 1)
            n0 = ATT_TILES
            for run, (tiles, blocks) in enumerate(RUNS):
                def group(i, k):
                    for u in range(k):
                        n = n0 + RING * i + u
                        if run == 0 and isinstance(i, int):
                            pool.wait_ge(w_begun, min(n - ATT_RING, ATT_TILES - 1) + 2)
                        else:
                            pool.wait_ge(w_begun, n - RING + 2)
                        loads = (n0 - ATT_TILES) // RAW_RING + (RING // RAW_RING) * i + u // RAW_RING + 1
                        r = u % RAW_RING
                        split(n, (n0 + u) % RING, r, RAW_RING, blocks, PAIRS + loads)
                group(0, RING)
                with pool.Fori(1, tiles // RING) as i:
                    group(i, RING)
                if tiles % RING:
                    group(tiles // RING, tiles % RING)
                n0 += tiles

        @block.tensor
        def _(pe):
            mm = nc.tensor.matmul

            def three(out, ah_, al_, bh_, bl_, start, stop, begins=False):
                first = mm(out, ah_, bh_, start=start, stop=False, skip_group_check=True)
                if begins:
                    first.then_inc(w_begun, 1)
                mm(out, ah_, bl_, start=False, stop=False, skip_group_check=True)
                return mm(out, al_, bh_, start=False, stop=stop, skip_group_check=True)

            def tile_ready(n):
                pe.wait_ge(w_low, n + 1)

            def blk(slot, b):
                return wh[:, slot, b * P:(b + 1) * P], wl[:, slot, b * P:(b + 1) * P]

            def x_blocks(slot, out, blocks, norm=None):
                for k in blocks:
                    if norm is not None:
                        pe.wait_ge(x_low, KC * norm + k + 1)
                    last = three(out, *blk(slot, k), xh[:, k, :], xl[:, k, :], k == 0, k == KC - 1,
                                 begins=k == 0)
                return last

            def stats(norm, by_token=False):
                pe.wait_ge(sumsq_low, norm + 1)
                mm(STAT[:], ones_r[:], sumsq_h[:], start=True, stop=False)
                mm(STAT[:], ones_r[:], sumsq_l[:], start=False, stop=True).then_inc(stat_done, 1)
                if by_token:
                    for b in range(TB):
                        cols = slice(b * P, (b + 1) * P)
                        mm(STAT_T[:, 2 * b:2 * b + 2], sumsq_h[:, cols], ones_r[:, 0:2], start=b == 0, stop=False,
                           skip_group_check=True)
                        last = mm(STAT_T[:, 2 * b:2 * b + 2], sumsq_l[:, cols], ones_r[:, 0:2], start=False,
                                  stop=True, skip_group_check=True)
                    last.then_inc(statT_done, 1)

            def qkv(p, which, blocks, norm=None):
                n, c = ATT_RING * p + which, 4 * p + which
                if 0 in blocks:
                    tile_ready(n)
                    if not isinstance(c, int) or c >= 2:
                        pe.wait_ge(chunk_freed, c - 1)
                last = x_blocks(which, bank[which % 2][:], blocks, norm)
                if KC - 1 in blocks:
                    last.then_inc(chunk_done, 1)

            def scores(p, half, par_):
                rows = slice(half * HD, (half + 1) * HD)
                s = 2 * p + half
                if half == 0:
                    pe.wait_ge(qk_low, 2 * p + 2)
                for jj, j in enumerate(reversed(range(TB))):
                    if not isinstance(s, int) or s >= 1:
                        pe.wait_ge(a_full, 4 * s - 4 + jj + 1)
                    keys = slice(j * P, (j + 1) * P)
                    z = Z[j][:, 0:T - j * P]
                    three(z, kh[rows, par_, keys], kl[rows, par_, keys], qh[rows, par_, j * P:T],
                          ql[rows, par_, j * P:T], True, False)
                    mm(z[:, 0:P], ident_r[:], maskneg[:], start=False, stop=True,
                       skip_group_check=True).then_inc(z_done, 1)

            def cumulate(s):
                for jj, j in enumerate(reversed(range(TB))):
                    pe.wait_ge(sp_low, 4 * s + jj + 1)
                    for j2 in range(j, TB):
                        left = negtri if j2 == j else negones
                        for part in (sph, spl):
                            last = mm(Z[j][:, (j2 - j) * P:T - j * P], left[:], part[j2][:], start=False,
                                      stop=True, skip_group_check=True)
                    last.then_inc(cum_done, 1)

            def values(s, half):
                pe.wait_ge(a_low, 4 * s + 4)
                if not isinstance(s, int) or s >= 2:
                    pe.wait_ge(o_low, s - 1)
                for j in range(TB):
                    last = three(O[half][:, j * P:T], vh[:, j, :], vl[:, j, :], ah[j][:], al[j][:], j == 0,
                                 j == TB - 1)
                last.then_inc(o_done, 1)

            def transpose_v(p):
                pe.wait_ge(chunk_freed, 4 * p + 3)
                for b in range(TB):
                    last = nc.tensor.transpose(bank[1][:, b * P:(b + 1) * P], vf[:, b * P:(b + 1) * P], ident[:])
                last.then_inc(chunk_done, 1)

            def attention_pair(p, par_, first=False, more=True):
                s = 2 * p
                low, high = range(KC // 2), range(KC // 2, KC)
                scores(p, 0, par_)
                if not first:
                    values(s - 1, 1)
                else:
                    pe.wait_ge(consts_ready, 6)
                transpose_v(p)
                if more:
                    qkv(p + 1, 0, range(KC))
                cumulate(s)
                if more:
                    qkv(p + 1, 1, low)
                scores(p, 1, par_)
                pe.wait_ge(chunk_freed, 4 * p + 4)
                values(s, 0)
                if more:
                    qkv(p + 1, 1, high)
                    qkv(p + 1, 2, low)
                cumulate(s + 1)
                if more:
                    qkv(p + 1, 2, high)

            pe.wait_ge(consts_ready, 5)
            qkv(0, 0, range(KC), 0)
            stats(0)
            qkv(0, 1, range(KC))
            qkv(0, 2, range(KC))
            attention_pair(0, 0, first=True)
            with pe.Fori(0, (PAIRS - 2) // 2) as i:
                attention_pair(2 * i + 1, 1)
                attention_pair(2 * i + 2, 0)
            attention_pair(PAIRS - 1, 1, more=False)
            values(HEADS - 1, 1)

            def bank_free(c):
                pe.wait_ge(chunk_freed, c - RING + 1)

            pe.wait_ge(chunk_freed, C_ATTOUT)
            with pe.Fori(0, KC // RING) as i:
                for u in range(RING):
                    n, c = N_ATTOUT + RING * i + u, C_ATTOUT + RING * i + u
                    tile_ready(n)
                    bank_free(c)
                    for p in range(PAIRS):
                        if u == 0:
                            pe.wait_ge(o_low, 2 * p + 2)
                        last = three(bank[u][:], *blk((N_ATTOUT + u) % RING, p), oh[:, p, :], ol[:, p, :], p == 0,
                                     p == PAIRS - 1, begins=p == 0)
                    last.then_inc(chunk_done, 1)

            def ffn_in(layer, norm):
                n0, c0 = N_FFN[layer], C_FFN[layer]

                def turn(i, first=False):
                    for u in range(RING):
                        tile_ready(n0 + RING * i + u)
                        bank_free(c0 + RING * i + u)
                        x_blocks((n0 + u) % RING, bank[u][:], range(KC), norm if first and u == 0 else None)\
                            .then_inc(chunk_done, 1)
                        if first and u == 0:
                            stats(norm)
                turn(0, True)
                with pe.Fori(1, FC // 2) as i:
                    turn(i)

            def ffn_out(layer):
                n0, c0 = N_FFNOUT[layer], C_FFNOUT[layer]
                with pe.Fori(0, KC // RING) as i:
                    for u in range(RING):
                        c = c0 + RING * i + u
                        bank_free(c)
                        for half in range(2):
                            n = n0 + 2 * (RING * i + u) + half
                            slot = (n0 + 2 * u + half) % RING
                            tile_ready(n)
                            for b in range(FH):
                                f = half * FH + b
                                if u == 0:
                                    pe.wait_ge(y_low, layer * FC + f + 1)
                                last = three(bank[u][:], *blk(slot, b), yh[:, f, :], yl[:, f, :], f == 0, f == FC - 1,
                                             begins=b == 0)
                        last.then_inc(chunk_done, 1)

            def embed(layer, norm):
                n0, c0 = N_PL[layer], C_PL[layer]
                for m in range(KC):
                    n = n0 + m // RING
                    if m % RING == 0:
                        tile_ready(n)
                    bank_free(c0 + m)
                    for q in range(PC):
                        if m == 0:
                            pe.wait_ge(p_low, PC * layer + q + 1)
                        last = three(bank[m % RING][:], *blk(n % RING, (m % RING) * PC + q), pinh[:, q, :],
                                     pinl[:, q, :], q == 0, q == PC - 1, begins=m % RING == 0 and q == 0)
                    last.then_inc(chunk_done, 1)
                stats(norm)
                n0 += KC * PC // W8
                for m in range(KC):
                    tile_ready(n0 + m)
                    bank_free(c0 + KC + m)
                    x_blocks((n0 + m) % RING, bank[m % RING][:], range(KC), norm if m == 0 else None)\
                        .then_inc(chunk_done, 1)

            def head_qk(n, c, first=False):
                for u in range(2 * RQC):
                    tile_ready(n + u)
                    bank_free(c + u)
                    x_blocks((N_RET + u) % RING, bank[u][:], range(KC), 3 if first and u == 0 else None)\
                        .then_inc(chunk_done, 1)
                    if first and u == 0:
                        stats(3, by_token=True)

            def head_v(n, c):
                for u in range(RING):
                    tile_ready(n + u)
                    slot = (N_RET + u) % RING
                    for kk in range(2):
                        k = 2 * u + kk
                        wide = slice(kk * RV, (kk + 1) * RV)
                        for b in range(TB):
                            if k == 0:
                                bank_free(c + b)
                            toks = slice(b * P, (b + 1) * P)
                            out = bank[b][:]
                            first_ = mm(out, xh[:, k, toks], wh[:, slot, wide], start=k == 0, stop=False,
                                        skip_group_check=True)
                            if kk == 0 and b == 0:
                                first_.then_inc(w_begun, 1)
                            mm(out, xh[:, k, toks], wl[:, slot, wide], start=False, stop=False, skip_group_check=True)
                            last = mm(out, xl[:, k, toks], wh[:, slot, wide], start=False, stop=k == KC - 1,
                                      skip_group_check=True)
                            if k == KC - 1:
                                last.then_inc(chunk_done, 1)

            def head_out(h, n, c):
                for m in range(KC):
                    t = m // 2
                    if m % 2 == 0:
                        tile_ready(n + t)
                    bank_free(c + m)
                    for e in range(RVC):
                        if m == 0:
                            pe.wait_ge(ry_low, RVC * h + e + 1)
                        last = three(bank[m % RING][:], *blk((N_RET + t) % RING, (m % 2) * RVC + e), ryh[:, e, :],
                                     ryl[:, e, :], e == 0, e == RVC - 1, begins=m % 2 == 0 and e == 0)
                    last.then_inc(chunk_done, 1)

            def head_scores(h, a):
                pe.wait_ge(rot_low, 2 * RQC * (h + 1))
                for j in range(TB):
                    if not isinstance(a, int) or a + j >= 2:
                        pe.wait_ge(aux_freed, a + j - 1)
                    keys = slice(j * P, (j + 1) * P)
                    for q in range(RQC):
                        last = three(AUX[j % 2][:, 0:T - j * P], rkh[:, q, keys], rkl[:, q, keys], rqh[:, q, j * P:T],
                                     rql[:, q, j * P:T], q == 0, q == RQC - 1)
                    last.then_inc(aux_done, 1)

            def head_g(n, c):
                for u in range(RVC):
                    tile_ready(n + u)
                    bank_free(c + u)
                    x_blocks((N_RET + u) % RING, bank[u][:], range(KC)).then_inc(chunk_done, 1)

            def head_values(h, c):
                pe.wait_ge(chunk_freed, c + TB)
                for b in range(TB):
                    g = TB * h + b
                    pe.wait_ge(s_low, g + 1)
                    if not isinstance(g, int) or g >= 2:
                        pe.wait_ge(ro_norm, g - 1)
                    for j in range(b + 1):
                        cols = slice((b - j) * P, (b - j + 1) * P)
                        last = three(O[b % 2][:], sh[j][:, cols], sl[j][:, cols], rvh[:, j, :], rvl[:, j, :],
                                     j == 0, j == b)
                    last.then_inc(ro_done, 1)

            def head_transpose(h, a):
                pe.wait_ge(ro_norm, TB * (h + 1))
                for e in range(RVC):
                    pe.wait_ge(aux_freed, a + e - 1)
                    for b in range(TB):
                        last = nc.tensor.transpose(AUX[e % 2][:, b * P:(b + 1) * P], on[:, b, e * P:(e + 1) * P],
                                                   ident[:])
                    last.then_inc(aux_done, 1)

            def retention():
                n, c = N_RET, C_RET
                head_qk(n, c, first=True)
                head_v(n + 4, c + 4)
                head_scores(0, 0)
                head_g(n + 8, c + 8)
                head_values(0, c + 4)
                n, c = n + 12, c + 12
                with pe.Fori(1, RH) as h:
                    nh, ch = n + HEAD_TILES * (h - 1), c + HEAD_CHUNKS * (h - 1)
                    head_qk(nh, ch)
                    head_transpose(h - 1, 8 * h - 4)
                    head_v(nh + 4, ch + 4)
                    head_out(h - 1, nh + 8, ch + 8)
                    head_scores(h, 8 * h)
                    head_g(nh + 12, ch + 16)
                    head_values(h, ch + 4)
                n, c = n + HEAD_TILES * (RH - 1), c + HEAD_CHUNKS * (RH - 1)
                head_transpose(RH - 1, 8 * RH - 4)
                head_out(RH - 1, n, c)

            ffn_in(0, 1)
            ffn_out(0)
            embed(0, 2)
            retention()
            ffn_in(1, 4)
            ffn_out(1)
            embed(1, 5)
            stats(6)

        @block.vector
        def _(dve):
            vec = nc.vector

            def low(out, full, high, done):
                vec.tensor_tensor(out, full, high.bitcast(F32), ALU.subtract).then_inc(done, 1)

            def norm_open(norm):
                if norm:
                    dve.wait_ge(sumsq_low, norm)
                vec.memset(sumsq[:], 0.0).then_inc(sumsq_zero, 1)

            def add_square(norm, k):
                at = KC * norm + k
                dve.wait_ge(sumsq_zero, norm + 1)
                dve.wait_ge(x_squared, at + 1)
                if not isinstance(at, int) or at >= 1:
                    dve.wait_ge(sq_added, at)
                vec.tensor_tensor(sumsq[:], sumsq[:], square[:], ALU.add).then_inc(sq_added, 1)

            def x_low_part(norm, k):
                at = KC * norm + k
                dve.wait_ge(x_high, at + 1)
                g = G_GAIN + norm * KC + k
                vec.scalar_tensor_tensor(one(xl, k), one(x, k), col(par, g), one(xh, k).bitcast(F32), ALU.mult,
                                         ALU.subtract).then_inc(x_low, 1)

            def norm_close(norm):
                dve.wait_ge(sq_added, KC * (norm + 1))
                vec.tensor_copy(sumsq_h[:], sumsq[:]).then_inc(sumsq_high, 1)
                dve.wait_ge(sumsq_high, norm + 1)
                low(sumsq_l[:], sumsq[:], sumsq_h[:], sumsq_low)

            def norm_scale(norm):
                dve.wait_ge(std_ready, norm + 1)
                vec.reciprocal(rstd[:], std[:]).then_inc(rstd_ready, 1)
                dve.wait_ge(rstd_ready, norm + 1)

            def x_add(c, u, k):
                dve.wait_ge(chunk_done, c + 1)
                vec.tensor_tensor(one(x, k), one(x, k), bank[u][:], ALU.add).then_inc(chunk_freed, 1)

            def x_phase(c0, norm):
                norm_open(norm)
                with dve.Fori(0, KC // RING) as i:
                    for u in range(RING):
                        k = RING * i + u
                        x_add(c0 + k, u, k)
                        x_low_part(norm, k)
                        add_square(norm, k)
                norm_close(norm)

            dve.wait_ge(par_loaded, 16)
            vec.memset(eps[:], EPS).then_inc(eps_ready, 1)
            norm_open(0)
            for k in range(KC):
                dve.wait_ge(x_loaded[k], 16)
                x_low_part(0, k)
                add_square(0, k)
            norm_close(0)
            dve.wait_ge(cst_loaded, 16)
            for out, at, factor in ((negtri, C_TRI, 1.0), (negones, C_ONES, 1.0), (ones_r, C_ONES, -1.0),
                                    (ident_r, C_IDENT, 1.0), (maskneg, C_MASK, 1.0), (ident, C_IDENT, 1.0)):
                vec.tensor_scalar(out[:], cst[:, at - C_TRI:at - C_TRI + P], factor, None, ALU.mult)\
                    .then_inc(consts_ready, 1)
            norm_scale(0)

            def take_qk(p, which, par_):
                c, at = 4 * p + which, 2 * p + which
                dve.wait_ge(chunk_done, c + 1)
                if not isinstance(at, int) or at >= 1:
                    dve.wait_ge(qk_low, at)
                vec.scalar_tensor_tensor(tmp[:], bank[which][:], HD ** -0.5 if which == 0 else 1.0, rstd[:],
                                         ALU.mult, ALU.mult).then_inc(chunk_freed, 1)
                dve.wait_ge(qk_high, at + 1)
                h_, l_ = ((qh, ql), (kh, kl))[which]
                low(l_[:, par_, :], tmp[:], h_[:, par_, :], qk_low)

            def take_v(p):
                dve.wait_ge(chunk_done, 4 * p + 3)
                vec.tensor_tensor(vf[:], bank[0][:], rstd[:], ALU.mult).then_inc(chunk_freed, 1)

            def take_vt(p):
                dve.wait_ge(vt_high, p + 1)
                low(vl[:].rearrange("p a t -> p (a t)"), bank[1][:], vh[:].rearrange("p a t -> p (a t)"),
                    chunk_freed)

            def take_o(s, p, half):
                rows = slice(half * HD, (half + 1) * HD)
                dve.wait_ge(o_high, s + 1)
                low(one(ol, p)[rows], O[half][rows, :], one(oh, p)[rows], o_low)

            def slot(p, half, par_, first=False, more=True):
                s = 2 * p + half
                if not first:
                    take_o(s - 1, p - (1 - half), 1 - half)
                if half == 0:
                    take_vt(p)

                def softplus(jj):
                    j = TB - 1 - jj
                    dve.wait_ge(z_ln, 4 * s + jj + 1)
                    vec.scalar_tensor_tensor(sp[j][:], Z[j][:, 0:T - j * P], 0.0, sp[j][:], ALU.max, ALU.add)\
                        .then_inc(sp_full, 1)

                def softplus_high(jj):
                    j = TB - 1 - jj
                    dve.wait_ge(sp_full, 4 * s + jj + 1)
                    vec.tensor_copy(sph[j][:], sp[j][:]).then_inc(sp_high, 1)

                def softplus_low(jj):
                    j = TB - 1 - jj
                    dve.wait_ge(sp_high, 4 * s + jj + 1)
                    low(spl[j][:], sp[j][:], sph[j][:], sp_low)

                def weights_high(jj):
                    j = TB - 1 - jj
                    dve.wait_ge(a_full, 4 * s + jj + 1)
                    vec.tensor_copy(ah[j][:], sp[j][:]).then_inc(a_high, 1)

                def weights_low(jj):
                    j = TB - 1 - jj
                    dve.wait_ge(a_high, 4 * s + jj + 1)
                    low(al[j][:], sp[j][:], ah[j][:], a_low)

                softplus(0)
                for jj in range(1, TB):
                    softplus_high(jj - 1)
                    softplus(jj)
                    softplus_low(jj - 1)
                softplus_high(TB - 1)
                softplus_low(TB - 1)
                if more:
                    take_qk(p + 1, half, 1 - par_)
                weights_high(0)
                for jj in range(1, TB):
                    weights_high(jj)
                    weights_low(jj - 1)
                weights_low(TB - 1)
                if more and half == 1:
                    take_v(p + 1)

            take_qk(0, 0, 0)
            take_qk(0, 1, 0)
            take_v(0)
            slot(0, 0, 0, first=True)
            slot(0, 1, 0)
            with dve.Fori(0, (PAIRS - 2) // 2) as i:
                for half in range(2):
                    slot(2 * i + 1, half, 1)
                for half in range(2):
                    slot(2 * i + 2, half, 0)
            slot(PAIRS - 1, 0, 1, more=False)
            slot(PAIRS - 1, 1, 1, more=False)
            take_o(HEADS - 1, PAIRS - 1, 1)
            x_phase(C_ATTOUT, 1)

            def ffn(layer, norm):
                c0 = C_FFN[layer]
                vec.memset(gate[:, :, 0:2], 0.0).then_inc(pads_ready, 1)
                norm_scale(norm)
                dve.wait_ge(pads_ready, layer + 1)
                with dve.Fori(0, FC // 2) as i:
                    for u in range(2):
                        f = 2 * i + u
                        at = layer * FC + f
                        c = c0 + 2 * f
                        g, cv = gate[:, u, :], conv[:, u, :]
                        w = [G_CONVW + (layer * CONV + tap) * FC + f for tap in range(CONV)]
                        dve.wait_ge(chunk_done, c + 1)
                        vec.tensor_tensor(g[:, 2:], bank[2 * u][:], rstd[:], ALU.mult).then_inc(chunk_freed, 1)
                        dve.wait_ge(chunk_freed, c + 1)
                        vec.tensor_scalar(cv, g[:, 2:], col(par, w[2]), col(par, G_CONVB + layer * FC + f), ALU.mult,
                                          ALU.add).then_inc(conv_step, 1)
                        for tap in (1, 0):
                            dve.wait_ge(conv_step, CONV * at + 2 - tap)
                            vec.scalar_tensor_tensor(cv, g[:, tap:tap + T], col(par, w[tap]), cv, ALU.mult,
                                                     ALU.add).then_inc(conv_step, 1)
                        dve.wait_ge(chunk_done, c + 2)
                        vec.tensor_tensor(up[:], bank[2 * u + 1][:], rstd[:], ALU.mult).then_inc(chunk_freed, 1)
                        dve.wait_ge(chunk_freed, c + 2)
                        dve.wait_ge(gate_silu, at + 1)
                        vec.tensor_tensor(yf[:], cv, up[:], ALU.mult).then_inc(y_full, 1)
                        dve.wait_ge(y_high, at + 1)
                        low(one(yl, f), yf[:], one(yh, f), y_low)
                for q in range(PC):
                    dve.wait_ge(p_high, layer * PC + q + 1)
                    low(pinl[:, q, :], pin[:, q, :], pinh[:, q, :], p_low)
                x_phase(C_FFNOUT[layer], norm + 1)

            def embed(layer, norm):
                c0 = C_PL[layer]
                with dve.Fori(0, KC // RING) as i:
                    for u in range(RING):
                        m = RING * i + u
                        dve.wait_ge(chunk_done, c0 + m + 1)
                        vec.tensor_copy(one(proj, m), bank[u][:]).then_inc(chunk_freed, 1)
                norm_scale(norm)
                norm_open(norm + 1)
                with dve.Fori(0, KC // RING) as i:
                    for u in range(RING):
                        m = RING * i + u
                        c, at = c0 + KC + m, layer * KC + m
                        dve.wait_ge(chunk_done, c + 1)
                        vec.tensor_tensor(gated[:, u % 2, :], bank[u][:], rstd[:], ALU.mult).then_inc(chunk_freed, 1)
                        dve.wait_ge(gate_open, at + 1)
                        vec.tensor_tensor(gated[:, u % 2, :], gated[:, u % 2, :], one(proj, m), ALU.mult)\
                            .then_inc(gate_times, 1)
                        dve.wait_ge(gate_times, at + 1)
                        vec.tensor_tensor(one(x, m), one(x, m), gated[:, u % 2, :], ALU.add).then_inc(x_new, 1)
                        add_square(norm + 1, m)
                norm_close(norm + 1)

            def take_rotated(h, c, which):
                a, b = bank[2 * which], bank[2 * which + 1]
                at = 2 * h + which
                dve.wait_ge(chunk_done, c + 2 * which + 2)
                if not isinstance(at, int) or at >= 1:
                    dve.wait_ge(rot_low, 2 * at)
                vec.tensor_tensor(rot[:, 0, :], a[:], cosr[:], ALU.mult).then_inc(rot_parts, 1)
                vec.tensor_tensor(rot[:, 1, :], b[:], sinr[:], ALU.mult).then_inc(rot_parts, 1)
                vec.tensor_tensor(rot[:, 2, :], a[:], sinr[:], ALU.mult).then_inc(chunk_freed, 1)
                vec.tensor_tensor(rot[:, 3, :], b[:], cosr[:], ALU.mult).then_inc(chunk_freed, 1)
                dve.wait_ge(rot_parts, 2 * at + 2)
                vec.tensor_tensor(rot[:, 0, :], rot[:, 0, :], rot[:, 1, :], ALU.subtract).then_inc(rot_full, 1)
                dve.wait_ge(chunk_freed, c + 2 * which + 2)
                vec.tensor_tensor(rot[:, 3, :], rot[:, 3, :], rot[:, 2, :], ALU.add).then_inc(rot_full, 1)
                h_, l_ = ((rqh, rql), (rkh, rkl))[which]
                for q in range(RQC):
                    dve.wait_ge(rot_high, 2 * at + q + 1)
                    low(l_[:, q, :], rot[:, 3 * q, :], h_[:, q, :], rot_low)

            def take_rv(h, c):
                for b in range(TB):
                    dve.wait_ge(rv_high, TB * h + b + 1)
                    vec.scalar_tensor_tensor(rvl[:, b, :], bank[b][:], rstdT[:, b, 0:1], rvh[:, b, :].bitcast(F32),
                                             ALU.mult, ALU.subtract).then_inc(chunk_freed, 1)

            def take_scores(h, a):
                for j in range(TB):
                    at = TB * h + j
                    dve.wait_ge(aux_done, a + j + 1)
                    if not isinstance(at, int) or at >= 1:
                        dve.wait_ge(s_low, at)
                    vec.tensor_tensor(sf[:, 0:T - j * P], AUX[j % 2][:, 0:T - j * P], one(decay, h)[:, 0:T - j * P],
                                      ALU.mult).then_inc(aux_freed, 1)
                    dve.wait_ge(s_high, at + 1)
                    low(sl[j][:], sf[:, 0:T - j * P], sh[j][:], s_low)

            def take_g(h, c):
                for u in range(RVC):
                    dve.wait_ge(chunk_done, c + u + 1)
                    vec.tensor_tensor(sg[:, u, :], bank[u][:], rstd[:], ALU.mult).then_inc(chunk_freed, 1)

            def group_norm(h):
                for b in range(TB):
                    g = TB * h + b
                    dve.wait_ge(ro_done, g + 1)
                    vec.bn_stats(st6[:, b, :], O[b % 2][:]).then_inc(ro_stat, 1)
                    dve.wait_ge(ro_stat, g + 1)
                    vec.memset(turn[:], 0.0)
                    vec.bn_aggr(st2[:, b, :], st6[:, b, :]).then_inc(ro_aggr, 1)
                    dve.wait_ge(ro_std, g + 1)
                    vec.reciprocal(grs[:, b:b + 1], gstd[:, b:b + 1]).then_inc(ro_rs, 1)
                    dve.wait_ge(ro_rs, g + 1)
                    vec.tensor_scalar(gnb[:, b:b + 1], st2[:, b, 0:1], grs[:, b:b + 1], -1.0, ALU.mult, ALU.mult)\
                        .then_inc(ro_nb, 1)

            def take_y(h, a):
                for e in range(RVC):
                    at = RVC * h + e
                    dve.wait_ge(aux_done, a + e + 1)
                    dve.wait_ge(g_silu, at + 1)
                    if not isinstance(at, int) or at >= 1:
                        dve.wait_ge(ry_low, at)
                    vec.tensor_tensor(ryf[:], AUX[e % 2][:], sg[:, e, :], ALU.mult).then_inc(aux_freed, 1)
                    dve.wait_ge(ry_high, at + 1)
                    low(ryl[:, e, :], ryf[:], ryh[:, e, :], ry_low)

            def retention():
                c = C_RET
                dve.wait_ge(tab_loaded, 32)
                vec.tensor_tensor(cosr[:], ang[:, 0, :], rstd[:], ALU.mult).then_inc(tab_scaled, 1)
                vec.tensor_tensor(sinr[:], ang[:, 1, :], rstd[:], ALU.mult).then_inc(tab_scaled, 1)
                dve.wait_ge(stdT_ready, 1)
                vec.reciprocal(rstdT[:], stdT[:]).then_inc(rstdT_ready, 1)
                dve.wait_ge(tab_scaled, 2)
                dve.wait_ge(rstdT_ready, 1)

                for which in range(2):
                    take_rotated(0, c, which)
                take_rv(0, c + 4)
                take_scores(0, 0)
                take_g(0, c + 8)
                group_norm(0)
                c += 12
                with dve.Fori(1, RH) as h:
                    ch = c + HEAD_CHUNKS * (h - 1)
                    for which in range(2):
                        take_rotated(h, ch, which)
                    take_y(h - 1, 8 * h - 4)
                    take_rv(h, ch + 4)
                    for m in range(KC):
                        x_add(ch + 8 + m, m % RING, m)
                    take_scores(h, 8 * h)
                    take_g(h, ch + 16)
                    group_norm(h)
                c += HEAD_CHUNKS * (RH - 1)
                take_y(RH - 1, 8 * RH - 4)
                x_phase(c, 4)

            ffn(0, 1)
            embed(0, 2)
            with dve.Fori(0, KC) as k:
                x_low_part(3, k)
            norm_scale(3)
            retention()
            ffn(1, 4)
            embed(1, 5)
            norm_scale(6)
            for m in range(KC):
                if m >= 2:
                    dve.wait_ge(out_stored[m % 2], 16 * (m // 2))
                vec.scalar_tensor_tensor(outt[:, m % 2, :], x[:, m, :], gain(6, m), rstd[:], ALU.mult, ALU.mult)\
                    .then_inc(out_ready, 1)

        @block.scalar
        def _(act):
            def copy(out, in_, done, scale=1.0):
                nc.scalar.activation(out, in_, ACT.Copy, bias=0.0, scale=scale).then_inc(done, 1)

            def x_square(norm, k):
                nc.scalar.activation(square[:], one(x, k), ACT.Square).then_inc(x_squared, 1)

            def last_square_added(norm, k):
                at = KC * norm + k
                if not isinstance(at, int) or at >= 1:
                    act.wait_ge(sq_added, at)

            def x_split(norm, k):
                last_square_added(norm, k)
                copy(one(xh, k), one(x, k), x_high, scale=col(par, G_GAIN + norm * KC + k))
                x_square(norm, k)

            def norm_std(norm):
                act.wait_ge(stat_done, norm + 1)
                nc.scalar.activation(std[:], STAT[:], ACT.Sqrt, bias=eps[:, 0:1], scale=1.0 / D).then_inc(std_ready, 1)

            def x_phase(c0, norm):
                with act.Fori(0, KC) as k:
                    act.wait_ge(chunk_freed, c0 + k + 1)
                    x_split(norm, k)

            act.wait_ge(par_loaded, 16)
            for k in range(KC):
                act.wait_ge(x_loaded[k], 16)
                x_split(0, k)
            act.wait_ge(eps_ready, 1)
            norm_std(0)

            def split_qk(p, which, par_):
                act.wait_ge(chunk_freed, 4 * p + which + 1)
                copy((qh, kh)[which][:, par_, :], tmp[:], qk_high)

            def slot(p, half, par_, first=False, more=True):
                s = 2 * p + half

                def magnitude(jj):
                    j = TB - 1 - jj
                    act.wait_ge(z_done, 4 * s + jj + 1)
                    nc.scalar.activation(sp[j][:], Z[j][:, 0:T - j * P], ACT.Abs).then_inc(z_abs, 1)

                def exp_negative(jj):
                    j = TB - 1 - jj
                    act.wait_ge(z_abs, 4 * s + jj + 1)
                    nc.scalar.activation(sp[j][:], sp[j][:], ACT.Exp, scale=-1.0).then_inc(z_exp, 1)

                def ln_one_plus(jj):
                    j = TB - 1 - jj
                    act.wait_ge(z_exp, 4 * s + jj + 1)
                    nc.scalar.activation(sp[j][:], sp[j][:], ACT.Ln, bias=1.0).then_inc(z_ln, 1)

                if not first:
                    act.wait_ge(a_low, 4 * s)
                magnitude(0)
                for jj in range(1, TB):
                    magnitude(jj)
                    exp_negative(jj - 1)
                exp_negative(TB - 1)
                if not first:
                    p_, half_ = p - (1 - half), 1 - half
                    rows = slice(half_ * HD, (half_ + 1) * HD)
                    act.wait_ge(o_done, s)
                    copy(one(oh, p_)[rows], O[half_][rows, :], o_high)
                if half == 0:
                    act.wait_ge(chunk_done, 4 * p + 4)
                    copy(vh[:].rearrange("p a t -> p (a t)"), bank[1][:], vt_high)
                for jj in range(TB):
                    ln_one_plus(jj)
                if more:
                    split_qk(p + 1, half, 1 - par_)
                for jj in range(TB):
                    j = TB - 1 - jj
                    act.wait_ge(cum_done, 4 * s + jj + 1)
                    nc.scalar.activation(sp[j][:], Z[j][:, 0:T - j * P], ACT.Exp).then_inc(a_full, 1)

            nc.scalar.preload_act_table_set("natural_log_exp_and_others")
            split_qk(0, 0, 0)
            split_qk(0, 1, 0)
            slot(0, 0, 0, first=True)
            slot(0, 1, 0)
            with act.Fori(0, (PAIRS - 2) // 2) as i:
                for half in range(2):
                    slot(2 * i + 1, half, 1)
                for half in range(2):
                    slot(2 * i + 2, half, 0)
            slot(PAIRS - 1, 0, 1, more=False)
            slot(PAIRS - 1, 1, 1, more=False)
            act.wait_ge(o_done, HEADS)
            copy(oh[HD:P, PAIRS - 1, :], O[1][HD:P, :], o_high)
            x_phase(C_ATTOUT, 1)

            def ffn(layer, norm):
                norm_std(norm)
                nc.scalar.preload_act_table(ACT.Silu)
                with act.Fori(0, FC // 2) as i:
                    for u in range(2):
                        f = 2 * i + u
                        at = layer * FC + f
                        act.wait_ge(conv_step, CONV * at + CONV)
                        nc.scalar.activation(conv[:, u, :], conv[:, u, :], ACT.Silu).then_inc(gate_silu, 1)
                        act.wait_ge(y_full, at + 1)
                        copy(one(yh, f), yf[:], y_high)
                act.wait_ge(y_low, FC * (layer + 1))
                act.dma_start(pin[:], pT[layer]).then_inc(p_loaded, 16)
                act.wait_ge(p_loaded, 16 * (layer + 1))
                for q in range(PC):
                    copy(pinh[:, q, :], pin[:, q, :], p_high)
                x_phase(C_FFNOUT[layer], norm + 1)

            def embed(layer, norm):
                norm_std(norm)
                nc.scalar.preload_act_table(ACT.Sigmoid)
                with act.Fori(0, KC // 2) as i:
                    for u in range(2):
                        m = 2 * i + u
                        act.wait_ge(chunk_freed, C_PL[layer] + KC + m + 1)
                        nc.scalar.activation(gated[:, u, :], gated[:, u, :], ACT.Sigmoid).then_inc(gate_open, 1)
                        last_square_added(norm + 1, m)
                        act.wait_ge(x_new, layer * KC + m + 1)
                        x_square(norm + 1, m)

            def split_rotated(h):
                for which in range(2):
                    for q in range(RQC):
                        at = 2 * RQC * h + RQC * which + q
                        act.wait_ge(rot_full, at + 1)
                        copy((rqh, rkh)[which][:, q, :], rot[:, 3 * q, :], rot_high)

            def split_rv(h, c):
                for b in range(TB):
                    act.wait_ge(chunk_done, c + b + 1)
                    copy(rvh[:, b, :], bank[b][:], rv_high, scale=rstdT[:, b, 0:1])

            def split_scores(h, a):
                for j in range(TB):
                    act.wait_ge(aux_freed, a + j + 1)
                    copy(sh[j][:], sf[:, 0:T - j * P], s_high)

            def silu_g(c):
                for u in range(RVC):
                    act.wait_ge(chunk_freed, c + u + 1)
                    nc.scalar.activation(sg[:, u, :], sg[:, u, :], ACT.Silu).then_inc(g_silu, 1)

            def group_norm(h):
                for b in range(TB):
                    g = TB * h + b
                    act.wait_ge(ro_aggr, g + 1)
                    nc.scalar.activation(gstd[:, b:b + 1], st2[:, b, 1:2], ACT.Sqrt, bias=eps[:, 0:1])\
                        .then_inc(ro_std, 1)
                    act.wait_ge(ro_nb, g + 1)
                    nc.scalar.activation(on[:, b, :], O[b % 2][:], ACT.Identity, bias=gnb[:, b:b + 1],
                                         scale=grs[:, b:b + 1]).then_inc(ro_norm, 1)

            def split_y(h, a):
                for e in range(RVC):
                    act.wait_ge(aux_freed, a + e + 1)
                    copy(ryh[:, e, :], ryf[:], ry_high)

            def retention():
                c = C_RET
                norm_std(3)
                act.wait_ge(statT_done, 1)
                nc.scalar.activation(stdT[:].rearrange("p a t -> p (a t)"), STAT_T[:, 0:2 * TB], ACT.Sqrt,
                                     bias=eps[:, 0:1], scale=1.0 / D).then_inc(stdT_ready, 1)
                split_rotated(0)
                act.wait_ge(rstdT_ready, 1)
                split_rv(0, c + 4)
                split_scores(0, 0)
                silu_g(c + 8)
                group_norm(0)
                c += 12
                with act.Fori(1, RH) as h:
                    ch = c + HEAD_CHUNKS * (h - 1)
                    split_rotated(h)
                    split_y(h - 1, 8 * h - 4)
                    split_rv(h, ch + 4)
                    split_scores(h, 8 * h)
                    silu_g(ch + 16)
                    group_norm(h)
                c += HEAD_CHUNKS * (RH - 1)
                split_y(RH - 1, 8 * RH - 4)
                x_phase(c, 4)

            ffn(0, 1)
            embed(0, 2)
            act.wait_ge(chunk_done, C_PL[0] + 2 * KC)
            act.dma_start(ang[:], consts[:, C_COS:C_DECAY].rearrange("p (a t) -> p a t", t=T)).then_inc(tab_loaded, 16)
            act.dma_start(decay[:], consts[:, C_DECAY:C_TRI].rearrange("p (a t) -> p a t", t=T))\
                .then_inc(tab_loaded, 16)
            with act.Fori(0, KC) as k:
                copy(one(xh, k), one(x, k), x_high, scale=col(par, G_GAIN + 3 * KC + k))
            retention()
            ffn(1, 4)
            embed(1, 5)
            norm_std(6)


def constants():
    half = RQK // 2
    inv = (np.float32(1.0) / np.power(np.float32(10000.0), np.arange(half, dtype=np.float32) / np.float32(half)))
    angle = inv.astype(np.float32)[:, None] * np.arange(T, dtype=np.float32)[None, :]
    c = np.zeros((P, C_COLS), np.float32)
    c[:, C_COS:C_COS + T] = np.cos(angle)
    c[:, C_SIN:C_SIN + T] = np.sin(angle)
    rel = np.arange(T)[None, :] - np.arange(P)[:, None]
    for h in range(RH):
        log_gamma = np.log1p(-np.exp2(-5.0 - h))
        c[:, C_DECAY + h * T:C_DECAY + (h + 1) * T] = np.where(rel >= 0, np.exp(log_gamma * np.maximum(rel, 0)), 0.0) * RQK ** -0.5
    key, col_ = np.arange(P)[:, None], np.arange(P)[None, :]
    c[:, C_TRI:C_TRI + P] = np.where(key >= col_, -1.0, 0.0)
    c[:, C_ONES:C_ONES + P] = -1.0
    c[:, C_IDENT:C_IDENT + P] = np.eye(P)
    c[:, C_MASK:C_MASK + P] = np.where(key >= col_, MASKED, 0.0)
    return c


def blocks(w):
    k, f = w.shape
    return w.reshape(k // P, P, f // P, P).transpose(2, 0, 1, 3)


def tiles(b):
    return b.transpose(0, 2, 1, 3).reshape(b.shape[0], P, -1)


def kernel(x, p, norm_mix, norm_ffn, norm_pl, norm_final, sb_w_in, sb_w_out, ret_w_in, ret_w_out,
           sgu_w_in, sgu_norm, sgu_w_s, sgu_b_s, sgu_w_out, ffn_w_in, ffn_conv_w, ffn_conv_b, ffn_w_out,
           pl_w_gate, pl_w_proj):
    import concourse.bacc as bacc
    from concourse.bass_utils import run_bass_kernel_spmd

    def ffn_tiles(layer):
        b = blocks(ffn_w_in[layer])
        both = np.stack([b[:FC], b[FC:]], axis=1).reshape(2 * FC, KC, P, P)
        out = blocks(ffn_w_out[layer]).reshape(2 * KC, FH, P, P)
        proj = blocks(pl_w_proj[layer]).reshape(KC * PC // W8, W8, P, P)
        return tiles(both), tiles(out), [tiles(proj), tiles(blocks(pl_w_gate[layer]))]

    qkv = blocks(sb_w_in[0]).reshape(3, PAIRS, KC, P, P).transpose(1, 0, 2, 3, 4).reshape(ATT_TILES, KC, P, P)
    ret = []
    w, wo = ret_w_in[0], ret_w_out[0]
    out_tiles = [tiles(blocks(wo[h * RV:(h + 1) * RV]).reshape(RVC, W8, P, P)) for h in range(RH)]
    for h in range(RH):
        qk = [blocks(w[:, o + h * RQK:o + (h + 1) * RQK]) for o in (0, D)]
        v = w[:, 2 * D + h * RV:2 * D + (h + 1) * RV].reshape(4, 2, P, RV).transpose(0, 2, 1, 3).reshape(4, P, 2 * RV)
        g = blocks(w[:, 4 * D + h * RV:4 * D + (h + 1) * RV])
        ret += [tiles(qk[0]), tiles(qk[1]), v] + ([out_tiles[h - 1]] if h else []) + [tiles(g)]
    ret.append(out_tiles[-1])
    (in0, out0, pl0), (in1, out1, pl1) = ffn_tiles(0), ffn_tiles(1)
    w8 = np.concatenate([tiles(qkv), tiles(blocks(sb_w_out[0])), in0, *pl0, *ret, in1, *pl1])
    w11 = np.concatenate([out0, out1])

    def by_chunk(v):
        return v.reshape(-1, P).T

    gains = np.stack([norm_mix[0], norm_ffn[0], norm_pl[0], norm_mix[1], norm_ffn[1], norm_pl[1], norm_final])
    params = np.concatenate([by_chunk(gains), by_chunk(ffn_conv_w), by_chunk(ffn_conv_b)], axis=1)
    arrays = {
        "xT": x[0].T.reshape(KC, P, T),
        "pT": p[:, 0].transpose(0, 2, 1).reshape(2, PC, P, T).transpose(0, 2, 1, 3),
        "w8": w8, "w11": w11, "params": params, "consts": constants(),
    }
    arrays = {n: np.ascontiguousarray(a) for n, a in arrays.items()}
    nc = bacc.Bacc("TRN2", target_bir_lowering=False, num_devices=1, dynamic_dma_scratch_size=DMA_SCRATCH)
    args = [nc.dram_tensor(f"in_{n}", a.shape, mybir.dt.from_np(a.dtype), kind="ExternalInput").ap()
            for n, a in arrays.items()]
    out = nc.dram_tensor("outT", (KC, P, T), F32, kind="ExternalOutput").ap()
    program(nc, *args, out)
    r = run_bass_kernel_spmd(nc, [{f"in_{n}": a for n, a in arrays.items()}], core_ids=[0])
    return r.results[0]["outT"].reshape(D, T).T[None]
```

```python
from contextlib import ExitStack

import numpy as np

import concourse.bass as bass
import concourse.mybir as mybir
from concourse.alu_op_type import AluOpType as ALU

ACT = mybir.ActivationFunctionType
F32 = mybir.dt.float32
F32R = mybir.dt.float32r

P = 128
D = 1024
T = 512
KC = D // P
TB = T // P
HEADS, HD = 16, 64
PAIRS = HEADS // 2
RH, RQK, RV = 4, 256, 512
RQC, RVC = RQK // P, RV // P
FF = 2816
FC = FF // P
FH = FC // 2
PL = 256
PC = PL // P
EPS = 1e-6
MASKED = -1e30
NORMS = 7
CONV = 3
DMA_SCRATCH = 256

ATT_TILES = 3 * PAIRS
W8 = 8
HEAD_TILES = 16
FFN_IN_TILES, FFN_OUT_TILES = 2 * FC, 2 * KC
PL_TILES = KC * PC // W8 + KC
RUNS = [
    (KC + FFN_IN_TILES, W8), (FFN_OUT_TILES, FH),
    (PL_TILES + RH * HEAD_TILES + FFN_IN_TILES, W8), (FFN_OUT_TILES, FH), (PL_TILES, W8)]
ATT_RING, RING, RAW_RING = 3, 4, 2
RAW_COLS = ATT_RING * W8 * P
assert RAW_RING * FH * P <= RAW_COLS

TILES = ATT_TILES + sum(n for n, _ in RUNS)
SLOTS = (0, 1, 3, 2)


def place(n):
    if n < ATT_TILES:
        return n % ATT_RING, n % ATT_RING, W8, n // ATT_RING + 1, max(n - ATT_RING + 2, 0)
    m, left = n - ATT_TILES, n - ATT_TILES
    for tiles_, blocks_ in RUNS:
        if left < tiles_:
            break
        left -= tiles_
    free = {0: n - 1, 1: n - 1, 2: n - 2, 3: n - 2}[m] if m < RING else n - RING + 2
    return SLOTS[m % RING], m % RAW_RING, blocks_, ATT_TILES // ATT_RING + m // RAW_RING + 1, free


def slot_of(n):
    return place(n)[0]


C_COS, C_SIN, C_DECAY = 0, T, 2 * T
C_TRI = C_DECAY + RH * T
C_ONES, C_IDENT, C_MASK = C_TRI + P, C_TRI + 2 * P, C_TRI + 3 * P
C_COLS = C_MASK + P
G_GAIN, G_CONVW = 0, NORMS * KC
G_CONVB = G_CONVW + 2 * CONV * FC
G_COLS = G_CONVB + 2 * FC


def program(nc, xT, pT, w8, w11, params, consts, outT):
    ctx = ExitStack()
    with ctx:
        def sb(name, shape, dt=F32, where=ctx):
            return where.enter_context(nc.sbuf_tensor(name, [P] + shape, dt))

        def sem(name):
            return ctx.enter_context(nc.semaphore(name))

        x = sb("x", [KC, T])
        xh, xl = sb("xh", [KC, T], F32R), sb("xl", [KC, T], F32R)
        raw = sb("raw", [RAW_COLS])
        wh, wl = sb("wh", [RING, FH * P], F32R), sb("wl", [RING, FH * P], F32R)
        par = sb("par", [G_COLS])
        eps, turn = sb("eps", [1]), sb("turn", [1])
        rstd, std, square = sb("rstd", [T]), sb("std", [T]), sb("square", [2, T])
        sumsq = sb("sumsq", [T])
        sumsq_h, sumsq_l = sb("sumsq_h", [T], F32R), sb("sumsq_l", [T], F32R)
        negtri, negones, ident_r, maskneg, ones_r = (
            sb(n, [P], F32R) for n in ("negtri", "negones", "ident_r", "maskneg", "ones_r"))
        ident = sb("ident", [P])

        with ExitStack() as ph:
            cst = sb("cst", [C_COLS - C_TRI], F32, ph)
            tmp = sb("att_tmp", [T], F32, ph)
            vf = sb("vf", [T], F32, ph)
            qh, ql, kh, kl = (sb(n, [2, T], F32R, ph) for n in ("qh", "ql", "kh", "kl"))
            vh, vl = sb("vh", [TB, P], F32R, ph), sb("vl", [TB, P], F32R, ph)
            sp = [sb(f"sp{j}", [T - j * P], F32, ph) for j in range(TB)]
            sph = [sb(f"sph{j}", [T - j * P], F32R, ph) for j in range(TB)]
            spl = [sb(f"spl{j}", [T - j * P], F32R, ph) for j in range(TB)]
            ah = [sb(f"ah{j}", [T - j * P], F32R, ph) for j in range(TB)]
            al = [sb(f"al{j}", [T - j * P], F32R, ph) for j in range(TB)]
            oh, ol = sb("oh", [PAIRS, T], F32R, ph), sb("ol", [PAIRS, T], F32R, ph)
        with ExitStack() as ph:
            gate = sb("gate", [2, T + 2], F32, ph)
            conv, up = sb("conv", [2, T], F32, ph), sb("up", [T], F32, ph)
            yf = sb("yf", [T], F32, ph)
            yh, yl = sb("yh", [FC, T], F32R, ph), sb("yl", [FC, T], F32R, ph)
        with ExitStack() as ph:
            pin = sb("pin", [PC, T], F32, ph)
            pinh, pinl = sb("pinh", [PC, T], F32R, ph), sb("pinl", [PC, T], F32R, ph)
            proj = sb("proj", [KC, T], F32, ph)
            gated = sb("gated", [2, T], F32, ph)
            outt = sb("outt", [2, T], F32, ph)
        with ExitStack() as ph:
            rotary = sb("rotary", [2, T], F32, ph)
            cosr, sinr = rotary[:, 0, :], rotary[:, 1, :]
            decay = sb("decay", [RH, T], F32, ph)
            stdT, rstdT = sb("stdT", [TB, 2], F32, ph), sb("rstdT", [TB, 2], F32, ph)
            rot = sb("rot", [4, T], F32, ph)
            rqh, rql, rkh, rkl = (sb(n, [RQC, T], F32R, ph) for n in ("rqh", "rql", "rkh", "rkl"))
            rvh, rvl = sb("rvh", [TB, RV], F32R, ph), sb("rvl", [TB, RV], F32R, ph)
            sf = sb("sf", [T], F32, ph)
            sh = [sb(f"sh{j}", [T - j * P], F32R, ph) for j in range(TB)]
            sl = [sb(f"sl{j}", [T - j * P], F32R, ph) for j in range(TB)]
            sg = sb("sg", [RVC, T], F32, ph)
            st6 = sb("st6", [TB, nc.vector.BN_STATS_DIM], F32, ph)
            st2 = sb("st2", [TB, nc.vector.BN_AGGR_DIM], F32, ph)
            gstd, grs, gnb = sb("gstd", [TB], F32, ph), sb("grs", [TB], F32, ph), sb("gnb", [TB], F32, ph)
            on = sb("on", [TB, RV], F32, ph)
            ryf = sb("ryf", [T], F32, ph)
            ryh, ryl = sb("ryh", [RVC, T], F32R, ph), sb("ryl", [RVC, T], F32R, ph)

        bank = [ctx.enter_context(nc.psum_tensor(f"bank{i}", [P, T], F32)) for i in range(8)]
        Z, O = bank[2:6], bank[6:8]
        AUX = bank[4:6]
        STAT, STAT_T = bank[4], bank[5]

        x_loaded = [sem(f"x_loaded{k}") for k in range(KC)]
        par_loaded, cst_loaded, p_loaded, tab_loaded = (
            sem(n) for n in ("par_loaded", "cst_loaded", "p_loaded", "tab_loaded"))
        w_loaded = [sem(f"w_loaded{r}") for r in range(ATT_RING)]
        w_high, w_low, w_begun = sem("w_high"), sem("w_low"), sem("w_begun")
        chunk_done, chunk_freed = sem("chunk_done"), sem("chunk_freed")
        consts_ready, eps_ready, pads_ready = sem("consts_ready"), sem("eps_ready"), sem("pads_ready")
        x_new, x_high, x_low, x_squared, sq_added, sumsq_zero = (
            sem(n) for n in ("x_new", "x_high", "x_low", "x_squared", "sq_added", "sumsq_zero"))
        sumsq_high, sumsq_low, stat_done, std_ready, rstd_ready = (
            sem(n) for n in ("sumsq_high", "sumsq_low", "stat_done", "std_ready", "rstd_ready"))
        statT_done, stdT_ready, rstdT_ready = sem("statT_done"), sem("stdT_ready"), sem("rstdT_ready")
        qk_high, qk_low, vt_high = sem("qk_high"), sem("qk_low"), sem("vt_high")
        z_done, z_abs, z_exp, z_ln = sem("z_done"), sem("z_abs"), sem("z_exp"), sem("z_ln")
        sp_full, sp_high, sp_low = sem("sp_full"), sem("sp_high"), sem("sp_low")
        cum_done, a_full, a_high, a_low = sem("cum_done"), sem("a_full"), sem("a_high"), sem("a_low")
        o_done, o_high, o_low = sem("o_done"), sem("o_high"), sem("o_low")
        conv_step, gate_silu, y_full, y_high, y_low = (
            sem(n) for n in ("conv_step", "gate_silu", "y_full", "y_high", "y_low"))
        p_high, p_low = sem("p_high"), sem("p_low")
        gate_open, gate_times = sem("gate_open"), sem("gate_times")
        tab_scaled, rot_parts, rot_full, rot_high, rot_low = (
            sem(n) for n in ("tab_scaled", "rot_parts", "rot_full", "rot_high", "rot_low"))
        rv_high = sem("rv_high")
        aux_done, aux_freed = sem("aux_done"), sem("aux_freed")
        s_high, s_low = sem("s_high"), sem("s_low")
        g_silu = sem("g_silu")
        ro_done, ro_stat, ro_aggr, ro_std, ro_rs, ro_nb, ro_norm = (
            sem(n) for n in ("ro_done", "ro_stat", "ro_aggr", "ro_std", "ro_rs", "ro_nb", "ro_norm"))
        ry_high, ry_low = sem("ry_high"), sem("ry_low")
        out_ready, out_stored = sem("out_ready"), [sem("out_stored0"), sem("out_stored1")]

        C_ATT = 0
        C_ATTOUT = 4 * PAIRS
        C_FFN = [C_ATTOUT + KC, 0]
        C_FFNOUT = [C_FFN[0] + 2 * FC, 0]
        C_PL = [C_FFNOUT[0] + KC, 0]
        C_RET = C_PL[0] + 2 * KC
        HEAD_CHUNKS = 2 * RQC + TB + KC + RVC
        C_FFN[1] = C_RET + RH * HEAD_CHUNKS
        C_FFNOUT[1] = C_FFN[1] + 2 * FC
        C_PL[1] = C_FFNOUT[1] + KC
        N_ATTOUT = ATT_TILES
        N_FFN = [N_ATTOUT + KC, 0]
        N_FFNOUT = [N_FFN[0] + FFN_IN_TILES, 0]
        N_PL = [N_FFNOUT[0] + FFN_OUT_TILES, 0]
        N_RET = N_PL[0] + PL_TILES
        N_FFN[1] = N_RET + RH * HEAD_TILES
        N_FFNOUT[1] = N_FFN[1] + FFN_IN_TILES
        N_PL[1] = N_FFNOUT[1] + FFN_OUT_TILES

        def gain(norm, k):
            at = G_GAIN + norm * KC + k
            return par[:, at:at + 1]

        def one(t, i):
            if isinstance(i, int):
                return t[:, i, :]
            return t[:, bass.ds(i, 1), :].rearrange("p a t -> p (a t)")

        def col(t, i):
            return t[:, i:i + 1] if isinstance(i, int) else t[:, bass.ds(i, 1)]

        block = ctx.enter_context(nc.Block())

        def raw_slot(ring, r, blocks):
            wide = RAW_COLS // ring
            return raw[:, r * wide:r * wide + blocks * P]

        @block.sync
        def _(sp_eng):
            def load(n, r, ring, blocks, src):
                sp_eng.dma_start(raw_slot(ring, r, blocks), src).then_inc(w_loaded[r], 16)

            sp_eng.dma_start(par[:], params).then_inc(par_loaded, 16)
            for k in range(KC):
                sp_eng.dma_start(x[:, k, :], xT[k]).then_inc(x_loaded[k], 16)
                if k < ATT_RING:
                    load(k, k, ATT_RING, W8, w8[k])
            sp_eng.dma_start(cst[:], consts[:, C_TRI:C_COLS]).then_inc(cst_loaded, 16)
            with sp_eng.Fori(1, PAIRS) as i:
                for u in range(ATT_RING):
                    sp_eng.wait_ge(w_low, ATT_RING * i + u - ATT_RING + 1)
                    load(0, u, ATT_RING, W8, w8[bass.ds(ATT_RING * i + u, 1)].rearrange("a p n -> (a p) n"))

            at8, at11, n0 = ATT_TILES, 0, ATT_TILES
            for run, (tiles, blocks) in enumerate(RUNS):
                src, at = (w8, at8) if blocks == W8 else (w11, at11)
                if run == 0:
                    sp_eng.wait_ge(w_low, ATT_TILES)
                def group(i, k):
                    for u in range(k):
                        n = n0 + RING * i + u
                        if not (run == 0 and isinstance(i, int) and u < RAW_RING):
                            sp_eng.wait_ge(w_low, n - RAW_RING + 1)
                        t = at + RING * i + u
                        load(n, u % RAW_RING, RAW_RING, blocks,
                             src[t] if isinstance(t, int) else src[bass.ds(t, 1)].rearrange("a p n -> (a p) n"))
                group(0, RING)
                with sp_eng.Fori(1, tiles // RING) as i:
                    group(i, RING)
                if tiles % RING:
                    group(tiles // RING, tiles % RING)
                n0 += tiles
                at8, at11 = (at8 + tiles, at11) if blocks == W8 else (at8, at11 + tiles)
            for m in range(KC):
                sp_eng.wait_ge(out_ready, m + 1)
                sp_eng.dma_start(outT[m], outt[:, m % 2, :]).then_inc(out_stored[m % 2], 16)
            for s in out_stored:
                sp_eng.wait_ge(s, 16 * KC // 2)

        @block.gpsimd
        def _(pool):
            def split_low(n, like):
                slot, r, blocks, _, _ = place(like)
                cols = slice(0, blocks * P)
                pool.wait_ge(w_high, n + 1)
                nc.gpsimd.tensor_tensor(wl[:, slot, cols], raw_slot(ATT_RING if like < ATT_TILES else RAW_RING, r, blocks),
                                        wh[:, slot, cols].bitcast(F32), ALU.subtract).then_inc(w_low, 1)

            with pool.Fori(0, PAIRS) as i:
                for u in range(ATT_RING):
                    split_low(ATT_RING * i + u, u)
            n0 = ATT_TILES
            for tiles, _ in RUNS:
                with pool.Fori(0, tiles // RING) as i:
                    for u in range(RING):
                        split_low(n0 + RING * i + u, n0 + u)
                for n in range(n0 + tiles // RING * RING, n0 + tiles):
                    split_low(n, n)
                n0 += tiles

        @block.tensor
        def _(pe):
            mm = nc.tensor.matmul

            def three(out, ah_, al_, bh_, bl_, start, stop, begins=False):
                first = mm(out, ah_, bh_, start=start, stop=False, skip_group_check=True)
                if begins:
                    first.then_inc(w_begun, 1)
                mm(out, ah_, bl_, start=False, stop=False, skip_group_check=True)
                return mm(out, al_, bh_, start=False, stop=stop, skip_group_check=True)

            def tile_ready(n):
                pe.wait_ge(w_low, n + 1)

            def blk(slot, b):
                return wh[:, slot, b * P:(b + 1) * P], wl[:, slot, b * P:(b + 1) * P]

            def x_blocks(slot, out, blocks, norm=None):
                for k in blocks:
                    if norm is not None:
                        pe.wait_ge(x_low, KC * norm + k + 1)
                    last = three(out, *blk(slot, k), xh[:, k, :], xl[:, k, :], k == 0, k == KC - 1,
                                 begins=k == 0)
                return last

            def stats(norm, by_token=False):
                pe.wait_ge(sumsq_low, norm + 1)
                mm(STAT[:], ones_r[:], sumsq_h[:], start=True, stop=False)
                mm(STAT[:], ones_r[:], sumsq_l[:], start=False, stop=True).then_inc(stat_done, 1)
                if by_token:
                    for b in range(TB):
                        cols = slice(b * P, (b + 1) * P)
                        mm(STAT_T[:, 2 * b:2 * b + 2], sumsq_h[:, cols], ones_r[:, 0:2], start=b == 0, stop=False,
                           skip_group_check=True)
                        last = mm(STAT_T[:, 2 * b:2 * b + 2], sumsq_l[:, cols], ones_r[:, 0:2], start=False,
                                  stop=True, skip_group_check=True)
                    last.then_inc(statT_done, 1)

            def qkv(p, which, blocks, norm=None):
                n, c = ATT_RING * p + which, 4 * p + which
                if 0 in blocks:
                    tile_ready(n)
                    if not isinstance(c, int) or c >= 2:
                        pe.wait_ge(chunk_freed, c - 1)
                last = x_blocks(which, bank[which % 2][:], blocks, norm)
                if KC - 1 in blocks:
                    last.then_inc(chunk_done, 1)

            def scores(p, half, par_):
                rows = slice(half * HD, (half + 1) * HD)
                s = 2 * p + half
                if half == 0:
                    pe.wait_ge(qk_low, 2 * p + 2)
                for jj, j in enumerate(reversed(range(TB))):
                    if not isinstance(s, int) or s >= 1:
                        pe.wait_ge(a_full, 4 * s - 4 + jj + 1)
                    keys = slice(j * P, (j + 1) * P)
                    z = Z[j][:, 0:T - j * P]
                    three(z, kh[rows, par_, keys], kl[rows, par_, keys], qh[rows, par_, j * P:T],
                          ql[rows, par_, j * P:T], True, False)
                    mm(z[:, 0:P], ident_r[:], maskneg[:], start=False, stop=True,
                       skip_group_check=True).then_inc(z_done, 1)

            def cumulate(s):
                for jj, j in enumerate(reversed(range(TB))):
                    pe.wait_ge(sp_low, 4 * s + jj + 1)
                    for j2 in range(j, TB):
                        left = negtri if j2 == j else negones
                        for part in (sph, spl):
                            last = mm(Z[j][:, (j2 - j) * P:T - j * P], left[:], part[j2][:], start=False,
                                      stop=True, skip_group_check=True)
                    last.then_inc(cum_done, 1)

            def values(s, half):
                pe.wait_ge(a_low, 4 * s + 4)
                if not isinstance(s, int) or s >= 2:
                    pe.wait_ge(o_low, s - 1)
                for j in range(TB):
                    last = three(O[half][:, j * P:T], vh[:, j, :], vl[:, j, :], ah[j][:], al[j][:], j == 0,
                                 j == TB - 1)
                last.then_inc(o_done, 1)

            def transpose_v(p):
                pe.wait_ge(chunk_freed, 4 * p + 3)
                for b in range(TB):
                    last = nc.tensor.transpose(bank[1][:, b * P:(b + 1) * P], vf[:, b * P:(b + 1) * P], ident[:])
                last.then_inc(chunk_done, 1)

            def attention_pair(p, par_, first=False, more=True):
                s = 2 * p
                low, high = range(KC // 2), range(KC // 2, KC)
                scores(p, 0, par_)
                if not first:
                    values(s - 1, 1)
                transpose_v(p)
                if more:
                    qkv(p + 1, 0, range(KC))
                cumulate(s)
                if more:
                    qkv(p + 1, 1, low)
                scores(p, 1, par_)
                pe.wait_ge(chunk_freed, 4 * p + 4)
                values(s, 0)
                if more:
                    qkv(p + 1, 1, high)
                    qkv(p + 1, 2, low)
                cumulate(s + 1)
                if more:
                    qkv(p + 1, 2, high)

            qkv(0, 0, range(KC), 0)
            pe.wait_ge(consts_ready, 6)
            stats(0)
            qkv(0, 1, range(KC))
            qkv(0, 2, range(KC))
            attention_pair(0, 0, first=True)
            with pe.Fori(0, (PAIRS - 2) // 2) as i:
                attention_pair(2 * i + 1, 1)
                attention_pair(2 * i + 2, 0)
            attention_pair(PAIRS - 1, 1, more=False)
            values(HEADS - 1, 1)

            def bank_free(c):
                pe.wait_ge(chunk_freed, c - RING + 1)

            pe.wait_ge(chunk_freed, C_ATTOUT)
            with pe.Fori(0, KC // RING) as i:
                for u in range(RING):
                    n, c = N_ATTOUT + RING * i + u, C_ATTOUT + RING * i + u
                    tile_ready(n)
                    bank_free(c)
                    for p in range(PAIRS):
                        if u == 0:
                            pe.wait_ge(o_low, 2 * p + 2)
                        last = three(bank[u][:], *blk(slot_of(N_ATTOUT + u), p), oh[:, p, :], ol[:, p, :], p == 0,
                                     p == PAIRS - 1, begins=p == 0)
                    last.then_inc(chunk_done, 1)

            def ffn_in(layer, norm):
                n0, c0 = N_FFN[layer], C_FFN[layer]

                def turn(i, first=False):
                    for u in range(RING):
                        tile_ready(n0 + RING * i + u)
                        bank_free(c0 + RING * i + u)
                        x_blocks(slot_of(n0 + u), bank[u][:], range(KC), norm if first and u == 0 else None)\
                            .then_inc(chunk_done, 1)
                        if first and u == 0:
                            stats(norm)
                turn(0, True)
                with pe.Fori(1, FC // 2) as i:
                    turn(i)

            def ffn_out(layer):
                n0, c0 = N_FFNOUT[layer], C_FFNOUT[layer]
                with pe.Fori(0, KC // RING) as i:
                    for u in range(RING):
                        c = c0 + RING * i + u
                        bank_free(c)
                        for half in range(2):
                            n = n0 + 2 * (RING * i + u) + half
                            slot = slot_of(n0 + 2 * u + half)
                            tile_ready(n)
                            for b in range(FH):
                                f = half * FH + b
                                if u == 0:
                                    pe.wait_ge(y_low, layer * FC + f + 1)
                                last = three(bank[u][:], *blk(slot, b), yh[:, f, :], yl[:, f, :], f == 0, f == FC - 1,
                                             begins=b == 0)
                        last.then_inc(chunk_done, 1)

            def embed(layer, norm):
                n0, c0 = N_PL[layer], C_PL[layer]
                for m in range(KC):
                    n = n0 + m // RING
                    if m % RING == 0:
                        tile_ready(n)
                    bank_free(c0 + m)
                    for q in range(PC):
                        if m == 0:
                            pe.wait_ge(p_low, PC * layer + q + 1)
                        last = three(bank[m % RING][:], *blk(slot_of(n), (m % RING) * PC + q), pinh[:, q, :],
                                     pinl[:, q, :], q == 0, q == PC - 1, begins=m % RING == 0 and q == 0)
                    last.then_inc(chunk_done, 1)
                stats(norm)
                n0 += KC * PC // W8
                for m in range(KC):
                    tile_ready(n0 + m)
                    bank_free(c0 + KC + m)
                    x_blocks(slot_of(n0 + m), bank[m % RING][:], range(KC), norm if m == 0 else None)\
                        .then_inc(chunk_done, 1)

            def head_qk(n, c, first=False):
                for u in range(2 * RQC):
                    tile_ready(n + u)
                    bank_free(c + u)
                    x_blocks(slot_of(N_RET + u), bank[u][:], range(KC), 3 if first and u == 0 else None)\
                        .then_inc(chunk_done, 1)
                    if first and u == 0:
                        stats(3, by_token=True)

            def head_v(n, c):
                for u in range(RING):
                    tile_ready(n + u)
                    slot = slot_of(N_RET + u)
                    for kk in range(2):
                        k = 2 * u + kk
                        wide = slice(kk * RV, (kk + 1) * RV)
                        for b in range(TB):
                            if k == 0:
                                bank_free(c + b)
                            toks = slice(b * P, (b + 1) * P)
                            out = bank[b][:]
                            first_ = mm(out, xh[:, k, toks], wh[:, slot, wide], start=k == 0, stop=False,
                                        skip_group_check=True)
                            if kk == 0 and b == 0:
                                first_.then_inc(w_begun, 1)
                            mm(out, xh[:, k, toks], wl[:, slot, wide], start=False, stop=False, skip_group_check=True)
                            last = mm(out, xl[:, k, toks], wh[:, slot, wide], start=False, stop=k == KC - 1,
                                      skip_group_check=True)
                            if k == KC - 1:
                                last.then_inc(chunk_done, 1)

            def head_out(h, n, c):
                for m in range(KC):
                    t = m // 2
                    if m % 2 == 0:
                        tile_ready(n + t)
                    bank_free(c + m)
                    for e in range(RVC):
                        if m == 0:
                            pe.wait_ge(ry_low, RVC * h + e + 1)
                        last = three(bank[m % RING][:], *blk(slot_of(N_RET + t), (m % 2) * RVC + e), ryh[:, e, :],
                                     ryl[:, e, :], e == 0, e == RVC - 1, begins=m % 2 == 0 and e == 0)
                    last.then_inc(chunk_done, 1)

            def head_scores(h, a):
                pe.wait_ge(rot_low, 2 * RQC * (h + 1))
                for j in range(TB):
                    if not isinstance(a, int) or a + j >= 2:
                        pe.wait_ge(aux_freed, a + j - 1)
                    keys = slice(j * P, (j + 1) * P)
                    for q in range(RQC):
                        last = three(AUX[j % 2][:, 0:T - j * P], rkh[:, q, keys], rkl[:, q, keys], rqh[:, q, j * P:T],
                                     rql[:, q, j * P:T], q == 0, q == RQC - 1)
                    last.then_inc(aux_done, 1)

            def head_g(n, c):
                for u in range(RVC):
                    tile_ready(n + u)
                    bank_free(c + u)
                    x_blocks(slot_of(N_RET + u), bank[u][:], range(KC)).then_inc(chunk_done, 1)

            def head_values(h, c):
                pe.wait_ge(chunk_freed, c + TB)
                for b in range(TB):
                    g = TB * h + b
                    pe.wait_ge(s_low, g + 1)
                    if not isinstance(g, int) or g >= 2:
                        pe.wait_ge(ro_norm, g - 1)
                    for j in range(b + 1):
                        cols = slice((b - j) * P, (b - j + 1) * P)
                        last = three(O[b % 2][:], sh[j][:, cols], sl[j][:, cols], rvh[:, j, :], rvl[:, j, :],
                                     j == 0, j == b)
                    last.then_inc(ro_done, 1)

            def head_transpose(h, a):
                pe.wait_ge(ro_norm, TB * (h + 1))
                for e in range(RVC):
                    pe.wait_ge(aux_freed, a + e - 1)
                    for b in range(TB):
                        last = nc.tensor.transpose(AUX[e % 2][:, b * P:(b + 1) * P], on[:, b, e * P:(e + 1) * P],
                                                   ident[:])
                    last.then_inc(aux_done, 1)

            def retention():
                n, c = N_RET, C_RET
                head_qk(n, c, first=True)
                head_v(n + 4, c + 4)
                head_scores(0, 0)
                head_g(n + 8, c + 8)
                head_values(0, c + 4)
                n, c = n + 12, c + 12
                with pe.Fori(1, RH) as h:
                    nh, ch = n + HEAD_TILES * (h - 1), c + HEAD_CHUNKS * (h - 1)
                    head_qk(nh, ch)
                    head_transpose(h - 1, 8 * h - 4)
                    head_v(nh + 4, ch + 4)
                    head_out(h - 1, nh + 8, ch + 8)
                    head_scores(h, 8 * h)
                    head_g(nh + 12, ch + 16)
                    head_values(h, ch + 4)
                n, c = n + HEAD_TILES * (RH - 1), c + HEAD_CHUNKS * (RH - 1)
                head_transpose(RH - 1, 8 * RH - 4)
                head_out(RH - 1, n, c)

            ffn_in(0, 1)
            ffn_out(0)
            embed(0, 2)
            retention()
            ffn_in(1, 4)
            ffn_out(1)
            embed(1, 5)
            stats(6)

        @block.vector
        def _(dve):
            vec = nc.vector

            def low(out, full, high, done):
                vec.tensor_tensor(out, full, high.bitcast(F32), ALU.subtract).then_inc(done, 1)

            def norm_open(norm):
                if norm:
                    dve.wait_ge(sumsq_low, norm)
                vec.memset(sumsq[:], 0.0).then_inc(sumsq_zero, 1)

            def add_square(norm, k, par_):
                at = KC * norm + k
                dve.wait_ge(sumsq_zero, norm + 1)
                dve.wait_ge(x_squared, at + 1)
                if not isinstance(at, int) or at >= 1:
                    dve.wait_ge(sq_added, at)
                vec.tensor_tensor(sumsq[:], sumsq[:], square[:, par_, :], ALU.add).then_inc(sq_added, 1)

            def x_low_part(norm, k):
                at = KC * norm + k
                dve.wait_ge(x_high, at + 1)
                g = G_GAIN + norm * KC + k
                vec.scalar_tensor_tensor(one(xl, k), one(x, k), col(par, g), one(xh, k).bitcast(F32), ALU.mult,
                                         ALU.subtract).then_inc(x_low, 1)

            def norm_close(norm):
                dve.wait_ge(sq_added, KC * (norm + 1))
                vec.tensor_copy(sumsq_h[:], sumsq[:]).then_inc(sumsq_high, 1)
                dve.wait_ge(sumsq_high, norm + 1)
                low(sumsq_l[:], sumsq[:], sumsq_h[:], sumsq_low)

            def norm_scale(norm):
                dve.wait_ge(std_ready, norm + 1)
                vec.reciprocal(rstd[:], std[:]).then_inc(rstd_ready, 1)
                dve.wait_ge(rstd_ready, norm + 1)

            def x_add(c, u, k):
                dve.wait_ge(chunk_done, c + 1)
                vec.tensor_tensor(one(x, k), one(x, k), bank[u][:], ALU.add).then_inc(chunk_freed, 1)

            def x_phase(c0, norm):
                norm_open(norm)
                with dve.Fori(0, KC // RING) as i:
                    for u in range(RING):
                        k = RING * i + u
                        x_add(c0 + k, u, k)
                        x_low_part(norm, k)
                        add_square(norm, k, u % 2)
                norm_close(norm)

            dve.wait_ge(par_loaded, 16)
            vec.memset(eps[:], EPS).then_inc(eps_ready, 1)
            norm_open(0)
            for k in range(KC):
                dve.wait_ge(x_loaded[k], 16)
                x_low_part(0, k)
            for k in range(KC):
                add_square(0, k, k % 2)
            norm_close(0)
            dve.wait_ge(cst_loaded, 16)
            for out, at, factor in ((negtri, C_TRI, 1.0), (negones, C_ONES, 1.0), (ones_r, C_ONES, -1.0),
                                    (ident_r, C_IDENT, 1.0), (maskneg, C_MASK, 1.0), (ident, C_IDENT, 1.0)):
                vec.tensor_scalar(out[:], cst[:, at - C_TRI:at - C_TRI + P], factor, None, ALU.mult)\
                    .then_inc(consts_ready, 1)
            norm_scale(0)

            def take_qk(p, which, par_):
                c, at = 4 * p + which, 2 * p + which
                dve.wait_ge(chunk_done, c + 1)
                if not isinstance(at, int) or at >= 1:
                    dve.wait_ge(qk_low, at)
                vec.scalar_tensor_tensor(tmp[:], bank[which][:], HD ** -0.5 if which == 0 else 1.0, rstd[:],
                                         ALU.mult, ALU.mult).then_inc(chunk_freed, 1)
                dve.wait_ge(qk_high, at + 1)
                h_, l_ = ((qh, ql), (kh, kl))[which]
                low(l_[:, par_, :], tmp[:], h_[:, par_, :], qk_low)

            def take_v(p):
                dve.wait_ge(chunk_done, 4 * p + 3)
                vec.tensor_tensor(vf[:], bank[0][:], rstd[:], ALU.mult).then_inc(chunk_freed, 1)

            def take_vt(p):
                dve.wait_ge(vt_high, p + 1)
                low(vl[:].rearrange("p a t -> p (a t)"), bank[1][:], vh[:].rearrange("p a t -> p (a t)"),
                    chunk_freed)

            def take_o(s, p, half):
                rows = slice(half * HD, (half + 1) * HD)
                dve.wait_ge(o_high, s + 1)
                low(one(ol, p)[rows], O[half][rows, :], one(oh, p)[rows], o_low)

            def slot(p, half, par_, first=False, more=True):
                s = 2 * p + half
                if not first:
                    take_o(s - 1, p - (1 - half), 1 - half)
                if half == 0:
                    take_vt(p)

                def softplus(jj):
                    j = TB - 1 - jj
                    dve.wait_ge(z_ln, 4 * s + jj + 1)
                    vec.scalar_tensor_tensor(sp[j][:], Z[j][:, 0:T - j * P], 0.0, sp[j][:], ALU.max, ALU.add)\
                        .then_inc(sp_full, 1)

                def softplus_high(jj):
                    j = TB - 1 - jj
                    dve.wait_ge(sp_full, 4 * s + jj + 1)
                    vec.tensor_copy(sph[j][:], sp[j][:]).then_inc(sp_high, 1)

                def softplus_low(jj):
                    j = TB - 1 - jj
                    dve.wait_ge(sp_high, 4 * s + jj + 1)
                    low(spl[j][:], sp[j][:], sph[j][:], sp_low)

                def weights_high(jj):
                    j = TB - 1 - jj
                    dve.wait_ge(a_full, 4 * s + jj + 1)
                    vec.tensor_copy(ah[j][:], sp[j][:]).then_inc(a_high, 1)

                def weights_low(jj):
                    j = TB - 1 - jj
                    dve.wait_ge(a_high, 4 * s + jj + 1)
                    low(al[j][:], sp[j][:], ah[j][:], a_low)

                softplus(0)
                for jj in range(1, TB):
                    softplus_high(jj - 1)
                    softplus(jj)
                    softplus_low(jj - 1)
                softplus_high(TB - 1)
                softplus_low(TB - 1)
                if more:
                    take_qk(p + 1, half, 1 - par_)
                weights_high(0)
                for jj in range(1, TB):
                    weights_high(jj)
                    weights_low(jj - 1)
                weights_low(TB - 1)
                if more and half == 1:
                    take_v(p + 1)

            take_qk(0, 0, 0)
            take_qk(0, 1, 0)
            take_v(0)
            slot(0, 0, 0, first=True)
            slot(0, 1, 0)
            with dve.Fori(0, (PAIRS - 2) // 2) as i:
                for half in range(2):
                    slot(2 * i + 1, half, 1)
                for half in range(2):
                    slot(2 * i + 2, half, 0)
            slot(PAIRS - 1, 0, 1, more=False)
            slot(PAIRS - 1, 1, 1, more=False)
            take_o(HEADS - 1, PAIRS - 1, 1)
            x_phase(C_ATTOUT, 1)

            def ffn(layer, norm):
                c0 = C_FFN[layer]
                vec.memset(gate[:, :, 0:2], 0.0).then_inc(pads_ready, 1)
                norm_scale(norm)
                dve.wait_ge(pads_ready, layer + 1)
                with dve.Fori(0, FC // 2) as i:
                    for u in range(2):
                        f = 2 * i + u
                        at = layer * FC + f
                        c = c0 + 2 * f
                        g, cv = gate[:, u, :], conv[:, u, :]
                        w = [G_CONVW + (layer * CONV + tap) * FC + f for tap in range(CONV)]
                        dve.wait_ge(chunk_done, c + 1)
                        vec.tensor_tensor(g[:, 2:], bank[2 * u][:], rstd[:], ALU.mult).then_inc(chunk_freed, 1)
                        dve.wait_ge(chunk_freed, c + 1)
                        vec.tensor_scalar(cv, g[:, 2:], col(par, w[2]), col(par, G_CONVB + layer * FC + f), ALU.mult,
                                          ALU.add).then_inc(conv_step, 1)
                        for tap in (1, 0):
                            dve.wait_ge(conv_step, CONV * at + 2 - tap)
                            vec.scalar_tensor_tensor(cv, g[:, tap:tap + T], col(par, w[tap]), cv, ALU.mult,
                                                     ALU.add).then_inc(conv_step, 1)
                        dve.wait_ge(chunk_done, c + 2)
                        vec.tensor_tensor(up[:], bank[2 * u + 1][:], rstd[:], ALU.mult).then_inc(chunk_freed, 1)
                        dve.wait_ge(chunk_freed, c + 2)
                        dve.wait_ge(gate_silu, at + 1)
                        vec.tensor_tensor(yf[:], cv, up[:], ALU.mult).then_inc(y_full, 1)
                        dve.wait_ge(y_high, at + 1)
                        low(one(yl, f), yf[:], one(yh, f), y_low)
                for q in range(PC):
                    dve.wait_ge(p_high, layer * PC + q + 1)
                    low(pinl[:, q, :], pin[:, q, :], pinh[:, q, :], p_low)
                x_phase(C_FFNOUT[layer], norm + 1)

            def embed(layer, norm):
                c0 = C_PL[layer]
                with dve.Fori(0, KC // RING) as i:
                    for u in range(RING):
                        m = RING * i + u
                        dve.wait_ge(chunk_done, c0 + m + 1)
                        vec.tensor_copy(one(proj, m), bank[u][:]).then_inc(chunk_freed, 1)
                norm_scale(norm)
                norm_open(norm + 1)
                with dve.Fori(0, KC // RING) as i:
                    for u in range(RING):
                        m = RING * i + u
                        c, at = c0 + KC + m, layer * KC + m
                        dve.wait_ge(chunk_done, c + 1)
                        vec.tensor_tensor(gated[:, u % 2, :], bank[u][:], rstd[:], ALU.mult).then_inc(chunk_freed, 1)
                        dve.wait_ge(gate_open, at + 1)
                        vec.tensor_tensor(gated[:, u % 2, :], gated[:, u % 2, :], one(proj, m), ALU.mult)\
                            .then_inc(gate_times, 1)
                        dve.wait_ge(gate_times, at + 1)
                        vec.tensor_tensor(one(x, m), one(x, m), gated[:, u % 2, :], ALU.add).then_inc(x_new, 1)
                        add_square(norm + 1, m, u % 2)
                norm_close(norm + 1)

            def take_rotated(h, c, which):
                a, b = bank[2 * which], bank[2 * which + 1]
                at = 2 * h + which
                dve.wait_ge(chunk_done, c + 2 * which + 2)
                if not isinstance(at, int) or at >= 1:
                    dve.wait_ge(rot_low, 2 * at)
                vec.tensor_tensor(rot[:, 0, :], a[:], cosr, ALU.mult).then_inc(rot_parts, 1)
                vec.tensor_tensor(rot[:, 1, :], b[:], sinr, ALU.mult).then_inc(rot_parts, 1)
                vec.tensor_tensor(rot[:, 2, :], a[:], sinr, ALU.mult).then_inc(chunk_freed, 1)
                vec.tensor_tensor(rot[:, 3, :], b[:], cosr, ALU.mult).then_inc(chunk_freed, 1)
                dve.wait_ge(rot_parts, 2 * at + 2)
                vec.tensor_tensor(rot[:, 0, :], rot[:, 0, :], rot[:, 1, :], ALU.subtract).then_inc(rot_full, 1)
                dve.wait_ge(chunk_freed, c + 2 * which + 2)
                vec.tensor_tensor(rot[:, 3, :], rot[:, 3, :], rot[:, 2, :], ALU.add).then_inc(rot_full, 1)
                h_, l_ = ((rqh, rql), (rkh, rkl))[which]
                for q in range(RQC):
                    dve.wait_ge(rot_high, 2 * at + q + 1)
                    low(l_[:, q, :], rot[:, 3 * q, :], h_[:, q, :], rot_low)

            def take_rv(h, c):
                for b in range(TB):
                    dve.wait_ge(rv_high, TB * h + b + 1)
                    vec.scalar_tensor_tensor(rvl[:, b, :], bank[b][:], rstdT[:, b, 0:1], rvh[:, b, :].bitcast(F32),
                                             ALU.mult, ALU.subtract).then_inc(chunk_freed, 1)

            def take_scores(h, a):
                for j in range(TB):
                    at = TB * h + j
                    dve.wait_ge(aux_done, a + j + 1)
                    if not isinstance(at, int) or at >= 1:
                        dve.wait_ge(s_low, at)
                    vec.tensor_tensor(sf[:, 0:T - j * P], AUX[j % 2][:, 0:T - j * P], one(decay, h)[:, 0:T - j * P],
                                      ALU.mult).then_inc(aux_freed, 1)
                    dve.wait_ge(s_high, at + 1)
                    low(sl[j][:], sf[:, 0:T - j * P], sh[j][:], s_low)

            def take_g(h, c):
                for u in range(RVC):
                    dve.wait_ge(chunk_done, c + u + 1)
                    vec.tensor_tensor(sg[:, u, :], bank[u][:], rstd[:], ALU.mult).then_inc(chunk_freed, 1)

            def group_norm(h):
                for b in range(TB):
                    g = TB * h + b
                    dve.wait_ge(ro_done, g + 1)
                    vec.bn_stats(st6[:, b, :], O[b % 2][:]).then_inc(ro_stat, 1)
                    dve.wait_ge(ro_stat, g + 1)
                    vec.memset(turn[:], 0.0)
                    vec.bn_aggr(st2[:, b, :], st6[:, b, :]).then_inc(ro_aggr, 1)
                    dve.wait_ge(ro_std, g + 1)
                    vec.reciprocal(grs[:, b:b + 1], gstd[:, b:b + 1]).then_inc(ro_rs, 1)
                    dve.wait_ge(ro_rs, g + 1)
                    vec.tensor_scalar(gnb[:, b:b + 1], st2[:, b, 0:1], grs[:, b:b + 1], -1.0, ALU.mult, ALU.mult)\
                        .then_inc(ro_nb, 1)

            def take_y(h, a):
                for e in range(RVC):
                    at = RVC * h + e
                    dve.wait_ge(aux_done, a + e + 1)
                    dve.wait_ge(g_silu, at + 1)
                    if not isinstance(at, int) or at >= 1:
                        dve.wait_ge(ry_low, at)
                    vec.tensor_tensor(ryf[:], AUX[e % 2][:], sg[:, e, :], ALU.mult).then_inc(aux_freed, 1)
                    dve.wait_ge(ry_high, at + 1)
                    low(ryl[:, e, :], ryf[:], ryh[:, e, :], ry_low)

            def retention():
                c = C_RET
                dve.wait_ge(tab_loaded, 32)
                vec.tensor_tensor(cosr, cosr, rstd[:], ALU.mult).then_inc(tab_scaled, 1)
                vec.tensor_tensor(sinr, sinr, rstd[:], ALU.mult).then_inc(tab_scaled, 1)
                dve.wait_ge(stdT_ready, 1)
                vec.reciprocal(rstdT[:], stdT[:]).then_inc(rstdT_ready, 1)
                dve.wait_ge(tab_scaled, 2)
                dve.wait_ge(rstdT_ready, 1)

                for which in range(2):
                    take_rotated(0, c, which)
                take_rv(0, c + 4)
                take_scores(0, 0)
                take_g(0, c + 8)
                group_norm(0)
                c += 12
                with dve.Fori(1, RH) as h:
                    ch = c + HEAD_CHUNKS * (h - 1)
                    for which in range(2):
                        take_rotated(h, ch, which)
                    take_y(h - 1, 8 * h - 4)
                    take_rv(h, ch + 4)
                    for m in range(KC):
                        x_add(ch + 8 + m, m % RING, m)
                    take_scores(h, 8 * h)
                    take_g(h, ch + 16)
                    group_norm(h)
                c += HEAD_CHUNKS * (RH - 1)
                take_y(RH - 1, 8 * RH - 4)
                x_phase(c, 4)

            ffn(0, 1)
            embed(0, 2)
            with dve.Fori(0, KC) as k:
                x_low_part(3, k)
            norm_scale(3)
            retention()
            ffn(1, 4)
            embed(1, 5)
            norm_scale(6)
            for m in range(KC):
                if m >= 2:
                    dve.wait_ge(out_stored[m % 2], 16 * (m // 2))
                vec.scalar_tensor_tensor(outt[:, m % 2, :], x[:, m, :], gain(6, m), rstd[:], ALU.mult, ALU.mult)\
                    .then_inc(out_ready, 1)

        @block.scalar
        def _(act):
            def copy(out, in_, done, scale=1.0):
                nc.scalar.activation(out, in_, ACT.Copy, bias=0.0, scale=scale).then_inc(done, 1)

            def tile_high(like, i=0, step=0):
                if like >= TILES:
                    return
                slot, r, blocks, loads, free = place(like)
                ring = ATT_RING if like < ATT_TILES else RAW_RING
                if free:
                    act.wait_ge(w_begun, free + step * i)
                act.wait_ge(w_loaded[r], 16 * loads + 16 * (step // ring) * i)
                copy(wh[:, slot, 0:blocks * P], raw_slot(ring, r, blocks), w_high)

            def square_free(norm, k):
                at = KC * norm + k
                if not isinstance(at, int) or at >= 2:
                    act.wait_ge(sq_added, at - 1)

            def x_square(norm, k, par_):
                nc.scalar.activation(square[:, par_, :], one(x, k), ACT.Square).then_inc(x_squared, 1)

            def x_high_part(norm, k):
                copy(one(xh, k), one(x, k), x_high, scale=col(par, G_GAIN + norm * KC + k))

            def norm_std(norm):
                act.wait_ge(stat_done, norm + 1)
                nc.scalar.activation(std[:], STAT[:], ACT.Sqrt, bias=eps[:, 0:1], scale=1.0 / D).then_inc(std_ready, 1)

            def x_chunk(c, norm, k, par_):
                square_free(norm, k)
                act.wait_ge(chunk_freed, c + 1)
                x_high_part(norm, k)
                x_square(norm, k, par_)

            for n in range(ATT_RING):
                if n == 1:
                    act.wait_ge(par_loaded, 16)
                    for k in range(KC):
                        act.wait_ge(x_loaded[k], 16)
                        x_high_part(0, k)
                tile_high(n)
            for k in range(KC):
                square_free(0, k)
                x_square(0, k, k % 2)
            act.wait_ge(eps_ready, 1)
            norm_std(0)
            nc.scalar.preload_act_table_set("natural_log_exp_and_others")

            def split_qk(p, which, par_):
                act.wait_ge(chunk_freed, 4 * p + which + 1)
                copy((qh, kh)[which][:, par_, :], tmp[:], qk_high)

            def slot(p, half, par_, first=False, more=True, v_tile=None, qk_tile=None):
                s = 2 * p + half

                def magnitude(jj):
                    j = TB - 1 - jj
                    act.wait_ge(z_done, 4 * s + jj + 1)
                    nc.scalar.activation(sp[j][:], Z[j][:, 0:T - j * P], ACT.Abs).then_inc(z_abs, 1)

                def exp_negative(jj):
                    j = TB - 1 - jj
                    act.wait_ge(z_abs, 4 * s + jj + 1)
                    nc.scalar.activation(sp[j][:], sp[j][:], ACT.Exp, scale=-1.0).then_inc(z_exp, 1)

                def ln_one_plus(jj):
                    j = TB - 1 - jj
                    act.wait_ge(z_exp, 4 * s + jj + 1)
                    nc.scalar.activation(sp[j][:], sp[j][:], ACT.Ln, bias=1.0).then_inc(z_ln, 1)

                if not first:
                    act.wait_ge(a_low, 4 * s)
                magnitude(0)
                for jj in range(1, TB):
                    magnitude(jj)
                    exp_negative(jj - 1)
                exp_negative(TB - 1)
                if not first:
                    p_, half_ = p - (1 - half), 1 - half
                    rows = slice(half_ * HD, (half_ + 1) * HD)
                    act.wait_ge(o_done, s)
                    copy(one(oh, p_)[rows], O[half_][rows, :], o_high)
                if half == 0:
                    act.wait_ge(chunk_done, 4 * p + 4)
                    copy(vh[:].rearrange("p a t -> p (a t)"), bank[1][:], vt_high)
                for jj in range(TB):
                    ln_one_plus(jj)
                if v_tile:
                    tile_high(*v_tile)
                if more:
                    split_qk(p + 1, half, 1 - par_)
                if qk_tile:
                    tile_high(*qk_tile)
                for jj in range(TB):
                    j = TB - 1 - jj
                    act.wait_ge(cum_done, 4 * s + jj + 1)
                    nc.scalar.activation(sp[j][:], Z[j][:, 0:T - j * P], ACT.Exp).then_inc(a_full, 1)

            def pair(p, par_, like, i=0, first=False):
                n, step = ATT_RING * like, 2 * ATT_RING
                slot(p, 0, par_, first, v_tile=(n + 5, i, step))
                tile_high(n + 6, i, step)
                slot(p, 1, par_, qk_tile=(n + 7, i, step))

            split_qk(0, 0, 0)
            tile_high(3)
            split_qk(0, 1, 0)
            tile_high(4)
            pair(0, 0, 0, first=True)
            with act.Fori(0, (PAIRS - 4) // 2) as i:
                pair(2 * i + 1, 1, 1, i)
                pair(2 * i + 2, 0, 2, i)
            pair(PAIRS - 3, 1, PAIRS - 3)
            pair(PAIRS - 2, 0, PAIRS - 2)
            slot(PAIRS - 1, 0, 1, more=False)
            tile_high(ATT_TILES + 2)
            slot(PAIRS - 1, 1, 1, more=False)
            act.wait_ge(o_done, HEADS)
            copy(oh[HD:P, PAIRS - 1, :], O[1][HD:P, :], o_high)
            tile_high(ATT_TILES + 3)
            with act.Fori(0, KC // RING) as i:
                for u in range(RING):
                    tile_high(N_ATTOUT + RING + u, i, RING)
                    x_chunk(C_ATTOUT + RING * i + u, 1, RING * i + u, u % 2)

            def ffn(layer, norm):
                n0, last = N_FFN[layer], FC // 2 - 1
                norm_std(norm)
                nc.scalar.preload_act_table(ACT.Silu)

                def turn(i, like, step):
                    for u in range(2):
                        f = 2 * i + u
                        at = layer * FC + f
                        tile_high(like + RING + 2 * u, i, step)
                        act.wait_ge(conv_step, CONV * at + CONV)
                        nc.scalar.activation(conv[:, u, :], conv[:, u, :], ACT.Silu).then_inc(gate_silu, 1)
                        tile_high(like + RING + 2 * u + 1, i, step)
                        act.wait_ge(y_full, at + 1)
                        copy(one(yh, f), yf[:], y_high)
                with act.Fori(0, last) as i:
                    turn(i, n0, RING)
                turn(last, n0 + RING * last, 0)
                act.wait_ge(y_low, FC * (layer + 1))
                act.dma_start(pin[:], pT[layer]).then_inc(p_loaded, 16)
                act.wait_ge(p_loaded, 16 * (layer + 1))
                for q in range(PC):
                    copy(pinh[:, q, :], pin[:, q, :], p_high)
                n0, last = N_FFNOUT[layer], KC // 2 - 1

                def out_turn(i, like, step):
                    for u in range(2):
                        tile_high(like + RING + 2 * u, i, step)
                        tile_high(like + RING + 2 * u + 1, i, step)
                        x_chunk(C_FFNOUT[layer] + 2 * i + u, norm + 1, 2 * i + u, u % 2)
                with act.Fori(0, last) as i:
                    out_turn(i, n0, RING)
                out_turn(last, n0 + RING * last, 0)

            def embed(layer, norm):
                n0, c0 = N_PL[layer] + KC * PC // W8, C_PL[layer] + KC
                tile_high(n0 + 2)
                norm_std(norm)
                tile_high(n0 + 3)
                nc.scalar.preload_act_table(ACT.Sigmoid)

                for i in range(KC // RING):
                    for u in range(RING):
                        m = RING * i + u
                        if not (layer == 0 and m == KC - 1):
                            tile_high(n0 + RING + m)
                        act.wait_ge(chunk_freed, c0 + m + 1)
                        nc.scalar.activation(gated[:, u % 2, :], gated[:, u % 2, :], ACT.Sigmoid).then_inc(gate_open, 1)
                        square_free(norm + 1, m)
                        act.wait_ge(x_new, layer * KC + m + 1)
                        x_square(norm + 1, m, u % 2)

            def head(h, c, like, i=0, first=False):
                step = 0 if first else HEAD_TILES

                def ahead(t):
                    tile_high(like + t + RING, i, step)

                if not first:
                    ahead(-1)
                for which in range(2):
                    if which == 0:
                        ahead(0)
                        ahead(1)
                    else:
                        ahead(2)
                    for q in range(RQC):
                        act.wait_ge(rot_full, 2 * RQC * h + RQC * which + q + 1)
                        copy((rqh, rkh)[which][:, q, :], rot[:, 3 * q, :], rot_high)
                if not first:
                    split_y(h - 1, 8 * h - 4)
                ahead(3)
                if first:
                    act.wait_ge(rstdT_ready, 1)
                for u in range(RING - 1):
                    ahead(4 + u)
                for b in range(TB):
                    act.wait_ge(chunk_done, c + 4 + b + 1)
                    copy(rvh[:, b, :], bank[b][:], rv_high, scale=rstdT[:, b, 0:1])
                t, cg = 8, c + 8
                if not first:
                    ahead(7)
                    for u in range(RING - 1):
                        ahead(8 + u)
                    t, cg = 12, c + 16
                for j in range(TB):
                    act.wait_ge(aux_freed, 8 * h + j + 1)
                    copy(sh[j][:], sf[:, 0:T - j * P], s_high)
                ahead(t - 1)
                for u in range(RVC):
                    act.wait_ge(chunk_freed, cg + u + 1)
                    nc.scalar.activation(sg[:, u, :], sg[:, u, :], ACT.Silu).then_inc(g_silu, 1)
                    if u < RVC - 1:
                        ahead(t + u)
                group_norm(h)

            def group_norm(h):
                for b in range(TB):
                    g = TB * h + b
                    act.wait_ge(ro_aggr, g + 1)
                    nc.scalar.activation(gstd[:, b:b + 1], st2[:, b, 1:2], ACT.Sqrt, bias=eps[:, 0:1])\
                        .then_inc(ro_std, 1)
                    act.wait_ge(ro_nb, g + 1)
                    nc.scalar.activation(on[:, b, :], O[b % 2][:], ACT.Identity, bias=gnb[:, b:b + 1],
                                         scale=grs[:, b:b + 1]).then_inc(ro_norm, 1)

            def split_y(h, a):
                for e in range(RVC):
                    act.wait_ge(aux_freed, a + e + 1)
                    copy(ryh[:, e, :], ryf[:], ry_high)

            def retention():
                c = C_RET
                norm_std(3)
                act.wait_ge(statT_done, 1)
                nc.scalar.activation(stdT[:].rearrange("p a t -> p (a t)"), STAT_T[:, 0:2 * TB], ACT.Sqrt,
                                     bias=eps[:, 0:1], scale=1.0 / D).then_inc(stdT_ready, 1)
                head(0, c, N_RET, first=True)
                with act.Fori(0, RH - 1) as i:
                    head(i + 1, c + 12 + HEAD_CHUNKS * i, N_RET + 12, i)
                n, c = N_FFN[1] - RING, c + 12 + HEAD_CHUNKS * (RH - 1)
                split_y(RH - 1, 8 * RH - 4)
                tile_high(n + RING - 1)
                for m in range(KC):
                    if m % 2 == 0:
                        tile_high(n + RING + m // 2)
                    x_chunk(c + m, 4, m, m % 2)

            ffn(0, 1)
            embed(0, 2)
            act.wait_ge(chunk_done, C_PL[0] + 2 * KC)
            act.dma_start(rotary[:], consts[:, C_COS:C_DECAY].rearrange("p (a t) -> p a t", t=T)).then_inc(tab_loaded, 16)
            act.dma_start(decay[:], consts[:, C_DECAY:C_TRI].rearrange("p (a t) -> p a t", t=T))\
                .then_inc(tab_loaded, 16)
            with act.Fori(0, KC) as k:
                copy(one(xh, k), one(x, k), x_high, scale=col(par, G_GAIN + 3 * KC + k))
            tile_high(N_RET + RING - 1)
            retention()
            ffn(1, 4)
            embed(1, 5)
            norm_std(6)


def constants():
    half = RQK // 2
    inv = (np.float32(1.0) / np.power(np.float32(10000.0), np.arange(half, dtype=np.float32) / np.float32(half)))
    angle = inv.astype(np.float32)[:, None] * np.arange(T, dtype=np.float32)[None, :]
    c = np.zeros((P, C_COLS), np.float32)
    c[:, C_COS:C_COS + T] = np.cos(angle)
    c[:, C_SIN:C_SIN + T] = np.sin(angle)
    rel = np.arange(T)[None, :] - np.arange(P)[:, None]
    for h in range(RH):
        log_gamma = np.log1p(-np.exp2(-5.0 - h))
        c[:, C_DECAY + h * T:C_DECAY + (h + 1) * T] = np.where(rel >= 0, np.exp(log_gamma * np.maximum(rel, 0)), 0.0) * RQK ** -0.5
    key, col_ = np.arange(P)[:, None], np.arange(P)[None, :]
    c[:, C_TRI:C_TRI + P] = np.where(key >= col_, -1.0, 0.0)
    c[:, C_ONES:C_ONES + P] = -1.0
    c[:, C_IDENT:C_IDENT + P] = np.eye(P)
    c[:, C_MASK:C_MASK + P] = np.where(key >= col_, MASKED, 0.0)
    return c


def blocks(w):
    k, f = w.shape
    return w.reshape(k // P, P, f // P, P).transpose(2, 0, 1, 3)


def tiles(b):
    return b.transpose(0, 2, 1, 3).reshape(b.shape[0], P, -1)


def kernel(x, p, norm_mix, norm_ffn, norm_pl, norm_final, sb_w_in, sb_w_out, ret_w_in, ret_w_out,
           sgu_w_in, sgu_norm, sgu_w_s, sgu_b_s, sgu_w_out, ffn_w_in, ffn_conv_w, ffn_conv_b, ffn_w_out,
           pl_w_gate, pl_w_proj):
    import concourse.bacc as bacc
    from concourse.bass_utils import run_bass_kernel_spmd

    def ffn_tiles(layer):
        b = blocks(ffn_w_in[layer])
        both = np.stack([b[:FC], b[FC:]], axis=1).reshape(2 * FC, KC, P, P)
        out = blocks(ffn_w_out[layer]).reshape(2 * KC, FH, P, P)
        proj = blocks(pl_w_proj[layer]).reshape(KC * PC // W8, W8, P, P)
        return tiles(both), tiles(out), [tiles(proj), tiles(blocks(pl_w_gate[layer]))]

    qkv = blocks(sb_w_in[0]).reshape(3, PAIRS, KC, P, P).transpose(1, 0, 2, 3, 4).reshape(ATT_TILES, KC, P, P)
    ret = []
    w, wo = ret_w_in[0], ret_w_out[0]
    out_tiles = [tiles(blocks(wo[h * RV:(h + 1) * RV]).reshape(RVC, W8, P, P)) for h in range(RH)]
    for h in range(RH):
        qk = [blocks(w[:, o + h * RQK:o + (h + 1) * RQK]) for o in (0, D)]
        v = w[:, 2 * D + h * RV:2 * D + (h + 1) * RV].reshape(4, 2, P, RV).transpose(0, 2, 1, 3).reshape(4, P, 2 * RV)
        g = blocks(w[:, 4 * D + h * RV:4 * D + (h + 1) * RV])
        ret += [tiles(qk[0]), tiles(qk[1]), v] + ([out_tiles[h - 1]] if h else []) + [tiles(g)]
    ret.append(out_tiles[-1])
    (in0, out0, pl0), (in1, out1, pl1) = ffn_tiles(0), ffn_tiles(1)
    w8 = np.concatenate([tiles(qkv), tiles(blocks(sb_w_out[0])), in0, *pl0, *ret, in1, *pl1])
    w11 = np.concatenate([out0, out1])

    def by_chunk(v):
        return v.reshape(-1, P).T

    gains = np.stack([norm_mix[0], norm_ffn[0], norm_pl[0], norm_mix[1], norm_ffn[1], norm_pl[1], norm_final])
    params = np.concatenate([by_chunk(gains), by_chunk(ffn_conv_w), by_chunk(ffn_conv_b)], axis=1)
    arrays = {
        "xT": x[0].T.reshape(KC, P, T),
        "pT": p[:, 0].transpose(0, 2, 1).reshape(2, PC, P, T).transpose(0, 2, 1, 3),
        "w8": w8, "w11": w11, "params": params, "consts": constants(),
    }
    arrays = {n: np.ascontiguousarray(a) for n, a in arrays.items()}
    nc = bacc.Bacc("TRN2", target_bir_lowering=False, num_devices=1, dynamic_dma_scratch_size=DMA_SCRATCH)
    args = [nc.dram_tensor(f"in_{n}", a.shape, mybir.dt.from_np(a.dtype), kind="ExternalInput").ap()
            for n, a in arrays.items()]
    out = nc.dram_tensor("outT", (KC, P, T), F32, kind="ExternalOutput").ap()
    program(nc, *args, out)
    r = run_bass_kernel_spmd(nc, [{f"in_{n}": a for n, a in arrays.items()}], core_ids=[0])
    return r.results[0]["outT"].reshape(D, T).T[None]
```
